# Optimizing a Trainium2 kernel written in Bass

```python
import math
import jax, jax.numpy as jnp
from jax import lax
import numpy as np

D_MODEL = 1024
BATCH = 1
SEQ = 256
DEPTH = 1
DEC_BATCH = 8
DEC_SEQ = 4
PAST_LEN = 2048
PAGE_SIZE = 128

D_PLE = 256
MIX_A = D_MODEL // 2
MIX_B = D_MODEL - MIX_A
H_A = 4
DV_A = MIX_A // H_A
DK_A = DV_A // 2
H_B = 4
DV_B = MIX_B // H_B
DK_B = DV_B
N_EXPERTS = 32
TOP_K = 4
D_FF = D_MODEL
SWIGLU_LIMIT = 7.0
SWIGLU_ALPHA = 1.702
CHUNK = 64
EXPERT_BLOCK = 128
LN_EPS = 1e-5
NORM_EPS = 1e-6
LB_FLOOR = 1e-20
DEEPNORM_ALPHA = (2 * DEPTH) ** 0.25
DEEPNORM_BETA = (8 * DEPTH) ** -0.25
SPLIT_SIZES = (H_A * DK_A, H_A * DK_A, MIX_A, MIX_A, H_A, H_A, H_B * DK_B, H_B * DK_B, MIX_B, MIX_B)
N_IN = sum(SPLIT_SIZES)
SPLIT_POINTS = tuple(int(s) for s in np.cumsum(SPLIT_SIZES)[:-1])

kernel_name = 'mlstm_hgrn2_moe_deepnorm_step'

def _layernorm(x, g, b):
    xf = x.astype(jnp.float32)
    mu = jnp.mean(xf, axis=-1, keepdims=True)
    var = jnp.mean(jnp.square(xf - mu), axis=-1, keepdims=True)
    y = (xf - mu) * lax.rsqrt(var + LN_EPS) * g.astype(jnp.float32) + b.astype(jnp.float32)
    return y.astype(x.dtype)

def _head_rmsnorm(h, g):
    H, Dv = h.shape[-2:]
    h = h * lax.rsqrt(jnp.mean(jnp.square(h), axis=-1, keepdims=True) + NORM_EPS)
    return h * g.astype(jnp.float32).reshape(H, Dv)

def _chunk_len(T):
    return CHUNK if T % CHUNK == 0 else T

def _to_chunks(a, L):
    B, T = a.shape[:2]
    return jnp.swapaxes(a.reshape((B, T // L, L) + a.shape[2:]), 0, 1)

def _from_chunks(a):
    nc, B, L = a.shape[:3]
    return jnp.swapaxes(a, 0, 1).reshape((B, nc * L) + a.shape[3:])

def _masked_exp(log_v, mask):
    return jnp.where(mask, jnp.exp(jnp.where(mask, log_v, 0.0)), 0.0)

def _mlstm_scan(q, k, v, i_log, f_log, C0, n0, m0):
    T = q.shape[1]
    L = _chunk_len(T)
    causal = jnp.tril(jnp.ones((L, L), dtype=bool))[None, :, :, None]

    def step(carry, xs):
        C, n, m = carry
        qc, kc, vc, ic, fc = xs
        b = jnp.cumsum(fc, axis=1)
        m_t = jnp.maximum(b + m[:, None], b + lax.cummax(ic - b, axis=1))
        inter = jnp.exp(b + m[:, None] - m_t)
        log_d = b[:, :, None] - b[:, None, :] + ic[:, None, :] - m_t[:, :, None]
        d = _masked_exp(log_d, causal)
        s = jnp.einsum('bthd,bshd->btsh', qc, kc) * d
        num = jnp.einsum('btsh,bshv->bthv', s, vc) + inter[..., None] * jnp.einsum('bthd,bhdv->bthv', qc, C)
        den = jnp.sum(s, axis=2) + inter * jnp.einsum('bthd,bhd->bth', qc, n)
        h = num / jnp.maximum(jnp.abs(den), jnp.exp(-m_t))[..., None]
        m_new = m_t[:, -1]
        w = jnp.exp(b[:, -1:] - b + ic - m_new[:, None])
        decay = jnp.exp(b[:, -1] + m - m_new)
        C = decay[..., None, None] * C + jnp.einsum('bsh,bshd,bshv->bhdv', w, kc, vc)
        n = decay[..., None] * n + jnp.einsum('bsh,bshd->bhd', w, kc)
        return (C, n, m_new), h

    xs = tuple(_to_chunks(a, L) for a in (q, k, v, i_log, f_log))
    (C, n, m), h = lax.scan(step, (C0, n0, m0), xs)
    return _from_chunks(h), C, n, m

def _hgrn2_scan(q, k, v, f_log, S0):
    T = q.shape[1]
    L = _chunk_len(T)
    causal = jnp.tril(jnp.ones((L, L), dtype=bool))[None, :, :, None, None]

    def step(S, xs):
        qc, kc, vc, fc = xs
        g = jnp.cumsum(fc, axis=1)
        dec = _masked_exp(g[:, :, None] - g[:, None, :], causal)
        a = jnp.sum(qc[:, :, None] * kc[:, None] * dec, axis=-1)
        o = jnp.einsum('btsh,bshv->bthv', a, vc) + jnp.einsum('bthd,bhdv->bthv', qc * jnp.exp(g), S)
        g_last = g[:, -1]
        S = jnp.exp(g_last)[..., None] * S + jnp.einsum('bshd,bshv->bhdv', kc * jnp.exp(g_last[:, None] - g), vc)
        return S, o

    xs = tuple(_to_chunks(a, L) for a in (q, k, v, f_log))
    S, o = lax.scan(step, S0, xs)
    return _from_chunks(o), S

def _mixer(x, C0, n0, m0, S0, w_in_l, ig_bias_l, fg_bias_l, norm_a_l, lb_l, norm_b_l, w_out_l):
    B, T, _ = x.shape
    f32 = jnp.float32
    proj = jnp.einsum('btd,dn->btn', x, w_in_l).astype(f32)
    qa, ka, va, oa, ia, fa, qb, fb, ib, gb = jnp.split(proj, SPLIT_POINTS, axis=-1)
    qa = qa.reshape(B, T, H_A, DK_A)
    ka = ka.reshape(B, T, H_A, DK_A) * (DK_A ** -0.5)
    va = va.reshape(B, T, H_A, DV_A)
    i_log = ia + ig_bias_l.astype(f32)
    f_log = jax.nn.log_sigmoid(fa + fg_bias_l.astype(f32))
    h_a, C, n, m = _mlstm_scan(qa, ka, va, i_log, f_log, C0.astype(f32), n0.astype(f32), m0.astype(f32))
    h_a = jax.nn.sigmoid(oa) * _head_rmsnorm(h_a, norm_a_l).reshape(B, T, MIX_A)
    lb = lb_l.reshape(H_B, DK_B)
    zf = fb.reshape(B, T, H_B, DK_B)
    f_log_b = jnp.logaddexp(jnp.log(jnp.maximum(lb, LB_FLOOR)), jnp.log1p(-lb) + jax.nn.log_sigmoid(zf))
    k_b = (1.0 - lb) * jax.nn.sigmoid(-zf)
    q_b = jax.nn.silu(qb).reshape(B, T, H_B, DK_B)
    v_b = ib.reshape(B, T, H_B, DV_B)
    o_b, S = _hgrn2_scan(q_b, k_b, v_b, f_log_b, S0.astype(f32))
    h_b = jax.nn.silu(gb) * _head_rmsnorm(o_b, norm_b_l).reshape(B, T, MIX_B)
    h = jnp.concatenate([h_a, h_b], axis=-1).astype(x.dtype)
    return h @ w_out_l, C, n, m, S

def _moe(x, w_router_l, b_router_l, wg, bg, wu, bu, wd, bd):
    B, T, D = x.shape
    n_tok = B * T
    xt = x.reshape(n_tok, D)
    logits = (xt @ w_router_l + b_router_l).astype(jnp.float32)
    top_v, top_i = lax.top_k(logits, TOP_K)
    gates = jax.nn.softmax(top_v, axis=-1)
    n_assign = n_tok * TOP_K
    e_flat = top_i.reshape(-1)
    order = jnp.argsort(e_flat)
    e_sorted = e_flat[order]
    tok_sorted = (order // TOP_K).astype(jnp.int32)
    gate_sorted = gates.reshape(-1)[order]
    counts = jnp.bincount(e_flat, length=N_EXPERTS)
    padded = (counts + EXPERT_BLOCK - 1) // EXPERT_BLOCK * EXPERT_BLOCK
    start = jnp.cumsum(counts) - counts
    pend = jnp.cumsum(padded)
    pstart = pend - padded
    dest = pstart[e_sorted] + jnp.arange(n_assign) - start[e_sorted]
    n_rows = -(-n_assign // EXPERT_BLOCK) * EXPERT_BLOCK + N_EXPERTS * EXPERT_BLOCK
    n_blocks = n_rows // EXPERT_BLOCK
    row_tok = jnp.zeros((n_rows,), jnp.int32).at[dest].set(tok_sorted)
    row_gate = jnp.zeros((n_rows,), jnp.float32).at[dest].set(gate_sorted)
    block_e = jnp.clip(jnp.searchsorted(pend, jnp.arange(n_blocks) * EXPERT_BLOCK, side='right'), 0, N_EXPERTS - 1)
    xin = xt[row_tok].reshape(n_blocks, EXPERT_BLOCK, D)

    def expert_block(args):
        xb, e = args
        gate = xb @ wg[e] + bg[e]
        up = xb @ wu[e] + bu[e]
        gate = jnp.minimum(gate, SWIGLU_LIMIT)
        up = jnp.clip(up, -SWIGLU_LIMIT, SWIGLU_LIMIT)
        glu = gate * jax.nn.sigmoid(gate * SWIGLU_ALPHA)
        return ((up + 1.0) * glu) @ wd[e] + bd[e]

    y_rows = lax.map(expert_block, (xin, block_e)).reshape(n_rows, D)
    y = jax.ops.segment_sum(y_rows.astype(jnp.float32) * row_gate[:, None], row_tok, num_segments=n_tok)
    return y.reshape(B, T, D).astype(x.dtype)

def setup_inputs(seed: int = 0) -> dict:
    key = jax.random.key(seed)
    ks = jax.random.split(key, 32)
    f32 = jnp.float32

    def nrm(k, shape, scale=1.0):
        return scale * jax.random.normal(k, shape, f32)

    return {
        'x_prompt': nrm(ks[0], (BATCH, SEQ, D_MODEL)),
        'x_sample': nrm(ks[1], (DEC_BATCH, DEC_SEQ, D_MODEL)),
        'state_mlstm_C': nrm(ks[2], (DEPTH, DEC_BATCH, H_A, DK_A, DV_A), 0.5),
        'state_mlstm_n': nrm(ks[3], (DEPTH, DEC_BATCH, H_A, DK_A), 0.5),
        'state_mlstm_m': nrm(ks[4], (DEPTH, DEC_BATCH, H_A)),
        'state_hgrn_S': nrm(ks[5], (DEPTH, DEC_BATCH, H_B, DK_B, DV_B), 0.5),
        'p_prompt': nrm(ks[6], (DEPTH, BATCH, SEQ, D_PLE)),
        'p_sample': nrm(ks[7], (DEPTH, DEC_BATCH, DEC_SEQ, D_PLE)),
        'ln_in_g': 1.0 + nrm(ks[8], (D_MODEL,), 0.02),
        'ln_in_b': nrm(ks[9], (D_MODEL,), 0.02),
        'w_in': nrm(ks[10], (DEPTH, D_MODEL, N_IN), D_MODEL ** -0.5),
        'mlstm_ig_bias': nrm(ks[11], (DEPTH, H_A), 0.1),
        'mlstm_fg_bias': jnp.linspace(3.0, 6.0, H_A, dtype=f32)[None, :] + nrm(ks[12], (DEPTH, H_A), 0.1),
        'mlstm_norm_g': 1.0 + nrm(ks[13], (DEPTH, MIX_A), 0.02),
        'hgrn_lb_logits': nrm(ks[14], (DEPTH, H_B * DK_B), 0.1),
        'hgrn_norm_g': 1.0 + nrm(ks[15], (DEPTH, MIX_B), 0.02),
        'w_out': nrm(ks[16], (DEPTH, D_MODEL, D_MODEL), DEEPNORM_BETA * D_MODEL ** -0.5),
        'ln1_g': 1.0 + nrm(ks[17], (DEPTH, D_MODEL), 0.02),
        'ln1_b': nrm(ks[18], (DEPTH, D_MODEL), 0.02),
        'w_router': nrm(ks[19], (DEPTH, D_MODEL, N_EXPERTS), D_MODEL ** -0.5),
        'b_router': nrm(ks[20], (DEPTH, N_EXPERTS), 0.01),
        'w_gate': nrm(ks[21], (DEPTH, N_EXPERTS, D_MODEL, D_FF), D_MODEL ** -0.5),
        'b_gate': nrm(ks[22], (DEPTH, N_EXPERTS, D_FF), 0.01),
        'w_up': nrm(ks[23], (DEPTH, N_EXPERTS, D_MODEL, D_FF), D_MODEL ** -0.5),
        'b_up': nrm(ks[24], (DEPTH, N_EXPERTS, D_FF), 0.01),
        'w_down': nrm(ks[25], (DEPTH, N_EXPERTS, D_FF, D_MODEL), DEEPNORM_BETA * D_FF ** -0.5),
        'b_down': nrm(ks[26], (DEPTH, N_EXPERTS, D_MODEL), 0.01),
        'w_ple_gate': nrm(ks[27], (DEPTH, D_MODEL, D_MODEL), D_MODEL ** -0.5),
        'w_ple_proj': nrm(ks[28], (DEPTH, D_PLE, D_MODEL), D_PLE ** -0.5),
        'ln2_g': 1.0 + nrm(ks[29], (DEPTH, D_MODEL), 0.02),
        'ln2_b': nrm(ks[30], (DEPTH, D_MODEL), 0.02),
    }

def reference(x_prompt, x_sample, state_mlstm_C, state_mlstm_n, state_mlstm_m, state_hgrn_S,
              p_prompt, p_sample, ln_in_g, ln_in_b, w_in, mlstm_ig_bias, mlstm_fg_bias,
              mlstm_norm_g, hgrn_lb_logits, hgrn_norm_g, w_out, ln1_g, ln1_b,
              w_router, b_router, w_gate, b_gate, w_up, b_up, w_down, b_down,
              w_ple_gate, w_ple_proj, ln2_g, ln2_b):
    f32 = jnp.float32
    lb_soft = jax.nn.softmax(hgrn_lb_logits.astype(f32), axis=0)
    lower_bounds = jnp.cumsum(lb_soft, axis=0) - lb_soft[0]

    def trunk(x, p, C_in, n_in, m_in, S_in):
        x = _layernorm(x, ln_in_g, ln_in_b)
        Cs, ns, ms, Ss = [], [], [], []
        for l in range(DEPTH):
            mix, C, n, m, S = _mixer(x, C_in[l], n_in[l], m_in[l], S_in[l], w_in[l], mlstm_ig_bias[l],
                                     mlstm_fg_bias[l], mlstm_norm_g[l], lower_bounds[l],
                                     hgrn_norm_g[l], w_out[l])
            x = _layernorm(DEEPNORM_ALPHA * x + mix, ln1_g[l], ln1_b[l])
            ple = jax.nn.sigmoid(x @ w_ple_gate[l]) * (p[l] @ w_ple_proj[l])
            ffn = _moe(x, w_router[l], b_router[l], w_gate[l], b_gate[l], w_up[l], b_up[l],
                       w_down[l], b_down[l])
            x = _layernorm(DEEPNORM_ALPHA * x + ffn + ple, ln2_g[l], ln2_b[l])
            Cs.append(C)
            ns.append(n)
            ms.append(m)
            Ss.append(S)
        return x, jnp.stack(Cs), jnp.stack(ns), jnp.stack(ms), jnp.stack(Ss)

    bp = x_prompt.shape[0]
    C_zero = jnp.zeros((DEPTH, bp, H_A, DK_A, DV_A), f32)
    n_zero = jnp.zeros((DEPTH, bp, H_A, DK_A), f32)
    m_zero = jnp.zeros((DEPTH, bp, H_A), f32)
    S_zero = jnp.zeros((DEPTH, bp, H_B, DK_B, DV_B), f32)
    y_prompt, C_p, n_p, m_p, S_p = trunk(x_prompt, p_prompt, C_zero, n_zero, m_zero, S_zero)
    y_sample, C_s, n_s, m_s, S_s = trunk(x_sample, p_sample, state_mlstm_C, state_mlstm_n,
                                         state_mlstm_m, state_hgrn_S)
    return (y_prompt, y_sample, C_p, n_p, m_p, S_p, C_s, n_s, m_s, S_s)


_drawn_inputs = setup_inputs


def setup_inputs(seed=0):
    import zlib

    import numpy as np

    out = dict(_drawn_inputs(seed))
    spreads = {}
    factors = {'mlstm_norm_g': 22.323,
     'hgrn_norm_g': 6.559,
     'b_router': 3.272,
     'b_gate': 24.919,
     'b_up': 36.112,
     'b_down': 8.0,
     'ln2_g': 8.433,
     'ln2_b': 8.03}
    for name, (base, spread) in spreads.items():
        noise = np.random.default_rng([zlib.crc32(name.encode()), seed]).standard_normal(out[name].shape)
        drawn = base * np.exp(spread * noise) if base else spread * noise
        out[name] = __import__('jax').numpy.asarray(drawn.astype(out[name].dtype))
    for name, factor in factors.items():
        out[name] = (out[name] * factor).astype(out[name].dtype)
    return out
```

```python
from contextlib import ExitStack

import numpy as np

import concourse.bass as bass
from concourse import mybir

F32 = mybir.dt.float32
BF16 = mybir.dt.bfloat16
I32 = mybir.dt.int32
U32 = mybir.dt.uint32
U8 = mybir.dt.uint8
ALU = mybir.AluOpType
ACT = mybir.ActivationFunctionType
AX_X = mybir.AxisListType.X

P = 128
D = 1024
KT = D // P
NP, NSEQ, TS = 256, 8, 4
NS = NSEQ * TS
NT = NP + NS
TILES = [(0, P), (P, P), (NP, NS)]
H = 4
DKA, DV = 64, 128
NE, TOPK = 32, 4
DPLE = 256
BLK = 64
NEXTRA = (NT * TOPK - 1) // BLK
NBLK = NE + NEXTRA
CHUNKS = [BLK * c for c in range(1, -(-NT // BLK))]
ALPHA = 2.0 ** 0.25
LN_EPS, NORM_EPS, LB_FLOOR = 1e-5, 1e-6, 1e-20
PLE_BLOCKS = KT
LIMIT, SWIGLU_ALPHA = 7.0, 1.702
LEVELS = [1, 2, 4, 8, 16, 32, 64]

RING = 12
W_GROUPS = [2056, 1544, 2568, 0, 512, 3080, 1024]
IF_COL = 1536
IN_SLOTS = 4 * len(W_GROUPS)
OUT_SLOT0 = IN_SLOTS
PRE = OUT_SLOT0 + KT
PER = 3 * KT
OUT_ORDER = [4, 5, 6, 7, 0, 1, 2, 3]

CF_IDENT, CF_ONES, CF_TRI, CF_HEAD, CF_PMOD, CF_IOTA, CF_SEQ = 0, 128, 256, 384, 896, 1024, 1088
CF_W = 1096


def constant_arrays():
    p = np.arange(P)[:, None]
    t = np.arange(P)[None, :]
    f = np.zeros((P, CF_W), np.float32)
    f[:, CF_IDENT:CF_IDENT + P] = p == t
    f[:, CF_ONES:CF_ONES + P] = 1.0
    f[:, CF_TRI:CF_TRI + P] = t >= p
    for h in range(H):
        f[h, CF_HEAD + h * P:CF_HEAD + (h + 1) * P] = 1.0
    f[:, CF_PMOD:CF_PMOD + BLK] = p % NE
    f[:, CF_IOTA:CF_IOTA + NE] = np.arange(NE)
    f[:, CF_IOTA + NE:CF_IOTA + 2 * NE] = np.arange(NE)
    f[:, CF_SEQ:CF_SEQ + NSEQ] = (p // TS) == np.arange(NSEQ)
    m = np.zeros((P, 2 + len(LEVELS), P), np.float32)
    m[:, 0] = p == t
    for n, half in enumerate(LEVELS):
        m[:, 1 + n] = (p // (2 * half) == t // (2 * half)) & (p % (2 * half) < half) & (t % (2 * half) >= half)
    m[:, 1 + len(LEVELS)] = (t >= p) & (p // TS == t // TS)
    tok = np.zeros((P, 3), np.int32)
    for i, (t0, r) in enumerate(TILES):
        tok[:r, i] = t0 + np.arange(r)
    return f, m.reshape(P, -1), tok


class Steps:

    def __init__(self, eng, sem):
        self.eng, self.sem, self.n = eng, sem, 0

    def __call__(self, ins):
        self.n += 1
        ins.then_inc(self.sem, 1)
        self.eng.wait_ge(self.sem, self.n)


def trunk_step(nc, a, o):
    x_rows = nc.dram_tensor("x_rows", (NT, D), F32, kind="Internal").ap()
    y_rows = nc.dram_tensor("y_rows", (NBLK * BLK, D), F32, kind="Internal").ap()
    slot_token = nc.dram_tensor("slot_token", (NBLK * BLK, 1), I32, kind="Internal").ap()

    w_in = a["w_in"][0].rearrange("(kt p) n -> p kt n", p=P)
    w_out = a["w_out"][0].rearrange("(kt p) n -> kt p n", p=P)
    w_pg = a["w_ple_gate"][0].rearrange("(kt p) n -> p kt n", p=P)
    w_pp = a["w_ple_proj"][0].rearrange("(kt p) n -> p kt n", p=P)
    w_ex = [a[n].rearrange("l e (kt p) n -> (l e) kt p n", p=P) for n in ("w_gate", "w_up", "w_down")]
    x_src = [a["x_prompt"][0, 0:P, :], a["x_prompt"][0, P:NP, :], a["x_sample"].rearrange("b t d -> (b t) d")]
    p_src = [a["p_prompt"][0, 0, 0:P, :], a["p_prompt"][0, 0, P:NP, :],
             a["p_sample"].rearrange("l b t d -> (l b t) d")]
    y_dst = [o[0][0, 0:P, :], o[0][0, P:NP, :], o[1].rearrange("b t d -> (b t) d")]

    with ExitStack() as ctx:
        def sb(name, shape, dt=F32):
            return ctx.enter_context(nc.sbuf_tensor(name, shape, dt))

        class Semaphores(dict):

            def __missing__(self, name):
                self[name] = ctx.enter_context(nc.semaphore(name))
                return self[name]

        S = Semaphores()
        slot_full = [S[f"slot_full{n}"] for n in range(RING)]

        ring = sb("ring", [P, RING, D])
        xs = sb("xs", [P, 3, D])
        ln_g, ln_b = sb("ln_g", [P, D]), sb("ln_b", [P, D])
        xT = sb("xT", [P, KT, NT])
        HT = xT
        cf = sb("cf", [P, CF_W])
        masks = sb("masks", [P, (2 + len(LEVELS)) * P], U8)
        tok_id = sb("tok_id", [P, 3], I32)
        eps = sb("eps", [P, 4])
        lns = sb("lns", [P, 2, 6])
        mv = sb("mv", [P, 4])
        w_if = sb("w_if", [P, KT, 2 * H])
        w_r = sb("w_r", [P, KT, NE])
        br = sb("br", [P, NE])
        G = sb("G", [P, H, NT])
        KB, QB = sb("KB", [P, H, NT]), sb("QB", [P, H, NT])
        GB, OA = sb("GB", [P, H, NT]), sb("OA", [P, H, NT])
        QK = sb("QK", [P, 4, NT])
        T = [sb(f"T{n}", [P, H, NT]) for n in range(4)]
        V = sb("V", [P, 3, D])
        AB, ABs = sb("AB", [P, H, 3, P]), sb("ABs", [NS, H, NS])
        AA, AAs = sb("AA", [P, H, 3, P]), sb("AAs", [NS, H, NS])
        S0 = sb("S0", [P, NSEQ, H, DV])
        C0 = sb("C0", [P, NSEQ, 2, DV])
        n0 = sb("n0", [P, 2, NSEQ])
        EM = sb("EM", [P, H, NT])
        rows = sb("rows", [H, 6, NT])
        r_bias = sb("r_bias", [H, 2])
        m0 = sb("m0", [H, 1 + NSEQ])
        r_start = sb("r_start", [H, 1 + NSEQ])
        cols = sb("cols", [P, 3, 2, H])
        inter = sb("inter", [P, 2, NS + NSEQ])
        decB = sb("decB", [P, H, NSEQ])
        qg = sb("qg", [P, H, NS])
        qi = sb("qi", [P, 2, NS])
        qn = sb("qn", [P, 2, NS])
        r_int = sb("r_int", [H, NS + NSEQ])
        gains = sb("gains", [P, 2, H])
        lb = sb("lb", [P, 6, H])
        logit = sb("logit", [P, NE])
        top_v = sb("top_v", [P, 3, 8])
        top_i = sb("top_i", [P, 3, 8], U32)
        top_f = sb("top_f", [P, 3, 8])
        neg_v = sb("neg_v", [P, 3])
        gsum = sb("gsum", [P, 3])
        gate = sb("gate", [P, 3, TOPK])
        oneh = sb("oneh", [P, 3, TOPK, NE])
        pick = sb("pick", [P, 3, NE])
        rank = sb("rank", [P, 3, NE])
        rt = sb("rt", [P, 2, 3, NE])
        ex = sb("ex", [P, 4, NE])
        pos = sb("pos", [P, 3, TOPK])
        pos_i = sb("pos_i", [P, 3, TOPK], I32)
        blk_e = sb("blk_e", [P, NBLK])
        blk_ei = sb("blk_ei", [P, NBLK], I32)
        ext = sb("ext", [P, NEXTRA, NE])
        n_exti = sb("n_exti", [P, 1], I32)
        zero_i = sb("zero_i", [NBLK, BLK], I32)
        bias3 = sb("bias3", [3 * NE, 3, D], BF16)
        sel = sb("sel", [3 * NE, BLK], BF16)
        sel2 = sb("sel2", [NE, D], BF16)
        idx = sb("idx", [BLK, 1], I32)

        def view(buf, start, size):
            flat = buf[:, :, :].rearrange("p a b -> p (a b)") if len(buf.shape) == 3 \
                else buf[:, :, :, :].rearrange("p a b c -> p (a b c)")
            return flat[:, start:start + size]

        reset = OA
        va_T = view(AA, 0, H * NT).rearrange("p (h t) -> p h t", h=H)
        VB = [view(b, 0, NSEQ * DV) for b in (T[1], T[2], QB, EM, GB)]
        KBt = view(AB, 0, 3 * 512).rearrange("p (i n) -> p i n", i=3)
        KAt = view(AA, 0, 3 * 256).rearrange("p (i n) -> p i n", i=3)
        sp_s, cp_s, np_s = view(T[3], 0, 512), view(T[3], 512, 256), view(T[3], 768, 2 + 2 * NSEQ)
        p_in = view(OA, 0, 3 * DPLE).rearrange("p (i d) -> p i d", i=3)
        pT = view(QK, 0, 2 * NT).rearrange("p (k t) -> p k t", k=2)
        ple_w = view(V, 0, 10 * P).rearrange("p (k n) -> p k n", k=10)
        ple = T[0][:, 0, :]
        x_g = view(G, 0, D)
        xTe = view(KB, 0, KT * BLK).rearrange("p (k s) -> p k s", k=KT)
        g_s, u_s = view(T[2], 0, 512), view(T[2], 512, 512)
        sg_s, h_s = view(EM, 0, 512), view(EM, 512, 512)
        hTe = view(QB, 0, 512).rearrange("p (j s) -> p j s", j=4)
        y_s = view(QB, 512, 512)

        ps = ctx.enter_context(nc.psum_tensor("ps", [P, 8, 512], F32))

        ident = cf[:, CF_IDENT:CF_IDENT + P]
        ones = cf[:, CF_ONES:CF_ONES + P]
        tri = cf[:, CF_TRI:CF_TRI + P]
        iota = cf[:, CF_IOTA:CF_IOTA + NE]
        seq_of = cf[0:NS, CF_SEQ:CF_SEQ + NSEQ]

        def head_row(h, n=P):
            return cf[0:H, CF_HEAD + h * P:CF_HEAD + h * P + n]

        def mask(n):
            return masks[:, n * P:(n + 1) * P]

        def scores(buf, part=P):
            return buf[0:part, :, 0:3:2, :]

        def flat(buf):
            return buf[:, :, :].rearrange("p h t -> p (h t)")

        def out_banks(i, half):
            r = TILES[i][1]
            if i < 2:
                return ps[0:r, 2 * i + half, :]
            return ps[64 * half:64 * half + r, 4, :]

        NLV = 2 + len(LEVELS)
        LVL_TILE = {12 + 2 * n: n for n in range(NLV)}
        NPROJ = 29
        ZROW = NEXTRA * BLK * D // (8 * P)
        N_VB = 2 * H

        block = ctx.enter_context(nc.Block())

        @block.sync
        def _(sp):
            used = [0]
            for i, (_, r) in enumerate(TILES):
                sp.dma_start(xs[0:r, i, :], x_src[i]).then_inc(S[f"x_in{i}"], 16)
            sp.dma_start(ln_g[:, :], a["ln_in_g"].partition_broadcast(P)).then_inc(S["ln1_in"], 16)
            sp.dma_start(ln_b[:, :], a["ln_in_b"].partition_broadcast(P)).then_inc(S["ln1_in"], 16)
            sp.dma_start(cf[:, :], a["const_f"]).then_inc(S["const_in"], 16)

            def ring_load(src, split):
                n, s = used[0], used[0] % RING
                if n >= RING:
                    sp.wait_ge(S["slots_used"], n - RING + 1)
                dst = ring[:, s, :].rearrange("p (k n) -> p k n", k=2) if split else ring[:, s, :]
                sp.dma_start(dst, src).then_inc(slot_full[s], 16)
                used[0] += 1

            for c0 in W_GROUPS:
                for q in range(4):
                    ring_load(w_in[:, 2 * q:2 * q + 2, c0:c0 + 512], True)
            for src in [w_out[k] for k in OUT_ORDER]:
                ring_load(src, False)

            def expert_weights(b, e, with_ple=False):
                order = [(w, k) for k in range(KT) for w in (0, 1)] + [(2, k) for k in range(KT)]
                for j, (w, k) in enumerate(order):
                    if with_ple and j == RING:
                        sp.wait_ge(S["ple_used"], b + 1)
                        sp.dma_start(ple_w[:, 0:KT, :], w_pg[:, :, bass.ds(b * P, P)]).then_inc(S["ple_w_in"], 16)
                        sp.dma_start(ple_w[:, KT:KT + 2, :], w_pp[:, :, bass.ds(b * P, P)]).then_inc(S["ple_w_in"], 16)
                    s = (PRE + j) % RING
                    sp.wait_ge(S["slots_used"], b * PER + (PRE + j - RING + 1))
                    sp.dma_start(ring[:, s, :],
                                 w_ex[w][bass.ds(e, 1), k, :, :].rearrange("e p n -> p (e n)")
                                 ).then_inc(slot_full[s], 16)

            with sp.Fori(0, PLE_BLOCKS) as b:
                expert_weights(b, b, True)
            with sp.Fori(PLE_BLOCKS, NE) as b:
                expert_weights(b, b)
            sp.wait_ge(S["pos_ok"], 1)
            extra = sp.value_load(n_exti[0:1, 0:1], min_val=0, max_val=NEXTRA)
            with sp.If(extra > 0):
                with sp.Fori(0, NEXTRA) as j:
                    with sp.If(extra > j):
                        e = sp.value_load(blk_ei[0:1, bass.ds(j + NE, 1)], min_val=0, max_val=NE - 1)
                        expert_weights(j + NE, e)
            for i, (_, r) in enumerate(TILES):
                sp.wait_ge(S["x_norm"], 7 + i)
                sp.dma_start(y_dst[i], xs[0:r, i, :]).then_inc(S["y_out"], 16)
            sp.wait_ge(S["y_out"], 48)

        @block.gpsimd
        def _(pool):
            with nc.allow_non_contiguous_dma(reason="small vectors laid out by partition"):
                for n, name in enumerate(("b_gate", "b_up", "b_down")):
                    pool.dma_start(view(T[n], 0, D)[0:NE, :], a[name][0]).then_inc(S["bias_in"], 16)
                pool.dma_start(flat(T[3]), a["const_m"]).then_inc(S["mask_in"], 16)
                pool.dma_start(lb[:, 0, :], a["hgrn_lb_logits"][0].rearrange("(h d) -> d h", d=P)).then_inc(S["vec_in"], 16)
                pool.dma_start(gains[:, 0, :], a["mlstm_norm_g"][0].rearrange("(h d) -> d h", d=P)).then_inc(S["vec_in"], 16)
                pool.dma_start(gains[:, 1, :], a["hgrn_norm_g"][0].rearrange("(h d) -> d h", d=P)).then_inc(S["vec_in"], 16)
                pool.dma_start(r_bias[:, 0:1], a["mlstm_ig_bias"].rearrange("l h -> h l")).then_inc(S["vec_in"], 16)
                pool.dma_start(r_bias[:, 1:2], a["mlstm_fg_bias"].rearrange("l h -> h l")).then_inc(S["vec_in"], 16)
                pool.dma_start(m0[:, 1:1 + NSEQ], a["state_mlstm_m"][0].rearrange("b h -> h b")).then_inc(S["vec_in"], 16)
                pool.dma_start(tok_id[:, :], a["const_t"]).then_inc(S["vec_in"], 16)
                pool.dma_start(w_if[:, :, :], w_in[:, :, IF_COL:IF_COL + 2 * H]).then_inc(S["if_in"], 16)
                pool.dma_start(S0[:, :, :, :].rearrange("p b h v -> p (b h) v"),
                               a["state_hgrn_S"][0].rearrange("b h d v -> d (b h) v")).then_inc(S["state_in"], 16)
                for h in range(H):
                    g, hh = h // 2, h % 2
                    pool.dma_start(C0[64 * hh:64 * hh + 64, :, g, :],
                                   a["state_mlstm_C"][0, :, h].rearrange("b d v -> d b v")).then_inc(S["state_in"], 16)
                    pool.dma_start(n0[64 * hh:64 * hh + 64, g, :],
                                   a["state_mlstm_n"][0, :, h].rearrange("b d -> d b")).then_inc(S["state_in"], 16)
                pool.dma_start(w_r[:, :, :], a["w_router"][0].rearrange("(kt p) n -> p kt n", p=P)).then_inc(S["router_in"], 16)
                pool.dma_start(br[:, :], a["b_router"][0].partition_broadcast(P)).then_inc(S["router_in"], 16)
                nc.gpsimd.memset(zero_i[:, :], 0).then_inc(S["zero_ok"], 1)
                pool.wait_ge(S["zero_ok"], 1)
                pool.dma_start(slot_token.rearrange("(b s) o -> b (s o)", s=BLK), zero_i[:, :]).then_inc(S["table_zero"], 16)
                pool.wait_ge(S["x_norm"], 3)
                pool.dma_start(ln_g[:, :], a["ln1_g"][0].partition_broadcast(P)).then_inc(S["ln2_in"], 16)
                pool.dma_start(ln_b[:, :], a["ln1_b"][0].partition_broadcast(P)).then_inc(S["ln2_in"], 16)

            pool.wait_ge(S["decB_ok"], 1)
            pool.wait_ge(S["inter_ok"], 1)
            pool.wait_ge(S["hA_ok"], 1)
            nc.gpsimd.tensor_tensor(S0[:, :, :, :], S0[:, :, :, :],
                                    decB[:, :, :].rearrange("p h b -> p b h").unsqueeze(3).to_broadcast([P, NSEQ, H, DV]),
                                    ALU.mult).then_inc(S["old_ok"], 1)
            dec_a = inter[:, :, NS:NS + NSEQ]
            nc.gpsimd.tensor_tensor(C0[:, :, :, :], C0[:, :, :, :],
                                    dec_a.rearrange("p g b -> p b g").unsqueeze(3).to_broadcast([P, NSEQ, 2, DV]),
                                    ALU.mult).then_inc(S["old_ok"], 1)
            nc.gpsimd.tensor_tensor(n0[:, :, :], n0[:, :, :], dec_a, ALU.mult).then_inc(S["old_ok"], 1)
            pool.wait_ge(S["mixed"], 2)
            for i, (_, r) in enumerate(TILES):
                pool.dma_start(p_in[0:r, i, :], p_src[i]).then_inc(S["p_in"], 16)
            for n in range(N_VB):
                if n >= len(VB):
                    pool.wait_ge(S["vb_used"], n - len(VB) + 1)
                off = 512 + n * DV if n < H else (n - H) * DV
                nc.gpsimd.tensor_tensor(VB[n % len(VB)][0:NS, :].rearrange("p (b v) -> p b v", b=NSEQ),
                                        V[0:NS, 2, off:off + DV].unsqueeze(1).to_broadcast([NS, NSEQ, DV]),
                                        seq_of.unsqueeze(2).to_broadcast([NS, NSEQ, DV]),
                                        ALU.mult).then_inc(S["vb_ok"], 1)
            pool.wait_ge(S["x_norm"], 6)
            pool.dma_start(ln_g[:, :], a["ln2_g"][0].partition_broadcast(P)).then_inc(S["ln3_in"], 16)
            pool.dma_start(ln_b[:, :], a["ln2_b"][0].partition_broadcast(P)).then_inc(S["ln3_in"], 16)

            pool.wait_ge(S["pos_ok"], 1)
            pool.wait_ge(S["table_zero"], 16)
            pool.wait_ge(S["vec_in"], 16 * 7)
            for i, (_, r) in enumerate(TILES):
                for k in range(TOPK):
                    pool.indirect_dma_start(slot_token, bass.IndirectOffsetOnAxis(ap=pos_i[0:r, i, k:k + 1], axis=0),
                                            tok_id[0:r, i:i + 1], None).then_inc(S["scat"], 16)
            pool.wait_ge(S["scat"], 16 * 3 * TOPK)
            pool.wait_ge(S["x1_rows"], 48)

            def gather(b):
                pool.wait_ge(S["xg_free"], b + 1)
                pool.dma_start(idx[:, :], slot_token[bass.ds(b * BLK, BLK), :]).then_inc(S["idx_full"], 16)
                pool.wait_ge(S["idx_full"], b * 16 + 16)
                pool.sem_inc(S["idx_seen"], 1)
                pool.indirect_dma_start(x_g[0:BLK, :], None, x_rows,
                                        bass.IndirectOffsetOnAxis(ap=idx[:, 0:1], axis=0)).then_inc(S["xg_full"], 16)
                pool.wait_ge(S["xg_full"], b * 16 + 16)

            with pool.Fori(0, NE) as b:
                gather(b)
            extra = pool.value_load(n_exti[0:1, 0:1], min_val=0, max_val=NEXTRA)
            with pool.If(extra > 0):
                with pool.Fori(0, NEXTRA) as j:
                    with pool.If(extra > j):
                        gather(j + NE)
            pool.wait_ge(S["y_done"], 1)
            pool.wait_ge(S["y_zero"], 16)
            for i, (_, r) in enumerate(TILES):
                for k in range(TOPK):
                    pool.indirect_dma_start(ring[0:r, i * TOPK + k, :], None, y_rows,
                                            bass.IndirectOffsetOnAxis(ap=pos_i[0:r, i, k:k + 1], axis=0)
                                            ).then_inc(S[f"picked{i}"], 16)

        @block.tensor
        def _(pe):
            slot = [0]
            mm = nc.tensor.matmul

            def slot_ready(n):
                pe.wait_ge(slot_full[n % RING], 16 * (n // RING + 1))

            pe.wait_ge(S["const_in"], 16)

            def transpose_x(i, first, bank0):
                r = TILES[i][1]
                for q in range(2):
                    n = first + 2 * i + q
                    if n >= 2:
                        pe.wait_ge(S["xT_ok"], n - 1)
                    dst = ps[:, bank0 + q, 0:4 * r].rearrange("p (k t) -> p k t", k=4)
                    for k in range(4):
                        c = 4 * q + k
                        last = nc.tensor.transpose(dst[:, k, :], xs[0:r, i, c * P:(c + 1) * P], ident[0:r, 0:r])
                    last.then_inc(S["xt_mm"], 1)

            for i in range(3):
                pe.wait_ge(S["x_norm"], i + 1)
                transpose_x(i, 0, 6)
            pe.wait_ge(S["xT_ok"], 6)

            def project(c, group, j):
                bank = c % 3
                if c >= 3:
                    pe.wait_ge(S["proj_ok"], c - 2)
                if group is None:
                    pe.wait_ge(S["if_in"], 16)
                    for k in range(KT):
                        mm(ps[0:H, bank, 0:NT], w_if[:, k, 0:H], xT[:, k, :], start=k == 0, stop=k == KT - 1)
                        last = mm(ps[32:32 + H, bank, 0:NT], w_if[:, k, H:2 * H], xT[:, k, :],
                                  start=k == 0, stop=k == KT - 1)
                    last.then_inc(S["proj_mm"], 1)
                    return
                for k in range(KT):
                    n = 4 * group + k // 2
                    if j == 0 and k % 2 == 0:
                        slot_ready(n)
                    w = ring[:, n % RING, (k % 2) * 512 + j * P:(k % 2) * 512 + (j + 1) * P]
                    last = mm(ps[:, bank, 0:NT], w, xT[:, k, :], start=k == 0, stop=k == KT - 1)
                    if k == KT - 1:
                        last.then_inc(S["proj_mm"], 1)
                    elif j == 3 and k % 2 == 1:
                        last.then_inc(S["slots_used"], 1)
                if j == 3:
                    pe.wait_ge(S["proj_mm"], c + 1)
                    pe.sem_inc(S["slots_used"], 1)

            def level(n):
                half = 1 << (n - 1) if n else 0
                src_k, src_q = (KB, QB) if n == 0 else (T[2 + n % 2], T[2 + n % 2])
                pe.wait_ge(S["mix_ok"], n + 1)
                if n:
                    pe.wait_ge(S["lvl_ok"], n)
                for h in range(H):
                    if n < NLV - 1:
                        for i in range(2):
                            c = (2 * h + i) * P
                            last = mm(ps[:, 3 + c // 512, c % 512:c % 512 + P], src_k[:, h, i * P:(i + 1) * P],
                                      src_q[:, h, i * P:(i + 1) * P], start=True, stop=True)
                        if half <= 2:
                            last = mm(ps[0:NS, 5, h * NS:(h + 1) * NS], src_k[:, h, NP:NT], src_q[:, h, NP:NT],
                                      start=True, stop=True)
                    else:
                        last = mm(ps[:, 3, h * P:(h + 1) * P], src_k[:, h, 0:P], src_q[:, h, P:NP],
                                  start=True, stop=True)
                last.then_inc(S["lvl_mm"], 1)

            def transpose_v(src, base):
                for i, (t0, r) in enumerate(TILES):
                    if base + i >= 2:
                        pe.wait_ge(S["v_ok"], base + i - 1)
                    for h in range(H):
                        last = nc.tensor.transpose(ps[0:r, 6 + (base + i) % 2, h * P:(h + 1) * P],
                                                   src[:, h, t0:t0 + r], ident)
                    last.then_inc(S["vt_mm"], 1)

            def gate_columns():
                pe.wait_ge(S["rows_ok"], 1)
                pe.wait_ge(S["lvl_ok"], 3)
                for i, (t0, r) in enumerate(TILES):
                    for q, row in enumerate((0, 2)):
                        nc.tensor.transpose(ps[0:r, 5, (2 * i + q) * H:(2 * i + q + 1) * H],
                                            rows[:, row, t0:t0 + r], ident[0:H, 0:H])
                for h in range(H):
                    g, hh = h // 2, h % 2
                    last = mm(ps[64 * hh:64 * hh + 64, 5, 64 + g * (NS + NSEQ):64 + (g + 1) * (NS + NSEQ)],
                              head_row(h, 64), r_int[:, :], start=True, stop=True)
                last.then_inc(S["rcol_mm"], 1)

            def spread_rows(h):
                pe.wait_ge(S["v_ok"], 6)
                if h:
                    pe.wait_ge(S["d_ok"], h)
                    pe.wait_ge(S["em_ok"], h)
                mm(ps[:, 6, 0:NT], head_row(h), rows[:, 5, :], start=True, stop=True)
                mm(ps[:, 7, 0:NT], head_row(h), rows[:, 1, :], start=True, stop=True).then_inc(S["rbc_mm"], 1)

            tiles = [(g, j) for g in range(3) for j in range(4)] + [(None, 0)] + \
                    [(g, j) for g in range(3, 7) for j in range(4)]
            assert len(tiles) == NPROJ
            for c, (g, j) in enumerate(tiles):
                project(c, g, j)
                if c == 13:
                    pe.wait_ge(S["proj_ok"], 12)
                    transpose_v(T[3], 0)
                if c == 19:
                    gate_columns()
                if c == 21:
                    pe.wait_ge(S["proj_ok"], 21)
                    transpose_v(va_T, 3)
                if 22 <= c < 26:
                    spread_rows(c - 22)
                if c in LVL_TILE:
                    level(LVL_TILE[c])
            slot[0] = IN_SLOTS

            pe.wait_ge(S["proj_ok"], NPROJ)
            pe.wait_ge(S["lvl_ok"], NLV)
            for h in range(H):
                g, lo = h // 2, 64 * (h % 2)
                q, k = QK[lo:lo + 64, g, :], QK[lo:lo + 64, 2 + g, :]
                mm(ps[:, h, 0:NP], k[:, 0:P], q[:, 0:NP], start=True, stop=True)
                mm(ps[:, h, NP:NP + P], k[:, P:NP], q[:, P:NP], start=True, stop=True)
                last = mm(ps[0:NS, h, 384:384 + NS], k[:, NP:NT], q[:, NP:NT], start=True, stop=True)
            last.then_inc(S["qk_mm"], 1)

            pe.wait_ge(S["d_ok"], H)
            pe.wait_ge(S["em_ok"], H)
            pe.wait_ge(S["qg_ok"], 1)
            pe.wait_ge(S["state_in"], 16 * 9)
            for h in range(H):
                out = ps[:, 4 + h, :]
                v = slice(512 + h * DV, 512 + (h + 1) * DV)
                mm(out[:, 0:NP], V[:, 0, v], AB[:, h, 0:2, :].rearrange("p i t -> p (i t)"), start=True, stop=False)
                mm(out[:, P:NP], V[:, 1, v], AB[:, h, 2, :], start=False, stop=False)
                mm(out[:, NP:NT], V[0:NS, 2, v], ABs[:, h, :], start=False, stop=False)
                for b in range(NSEQ):
                    last = mm(out[:, NP + b * TS:NP + (b + 1) * TS], S0[:, b, h, :], qg[:, h, b * TS:(b + 1) * TS],
                              start=False, stop=b == NSEQ - 1)
            last.then_inc(S["oB_mm"], 1)

            pe.wait_ge(S["sA_ok"], 1)
            pe.wait_ge(S["inter_ok"], 1)
            for h in range(H):
                g, lo = h // 2, 64 * (h % 2)
                out = ps[:, h, :]
                v = slice(h * DV, (h + 1) * DV)
                mm(out[:, 0:NP], V[:, 0, v], AA[:, h, 0:2, :].rearrange("p i t -> p (i t)"), start=True, stop=False)
                mm(out[:, P:NP], V[:, 1, v], AA[:, h, 2, :], start=False, stop=False)
                mm(out[:, NP:NT], V[0:NS, 2, v], AAs[:, h, :], start=False, stop=False)
                for b in range(NSEQ):
                    last = mm(out[:, NP + b * TS:NP + (b + 1) * TS], C0[lo:lo + 64, b, g, :],
                              qi[lo:lo + 64, g, b * TS:(b + 1) * TS], start=False, stop=b == NSEQ - 1)
            last.then_inc(S["numA_mm"], 1)

            pe.wait_ge(S["oB_sq"], 1)
            for h in range(H):
                last = mm(ps[:, 4 + h, 0:NT], ones, T[1][:, h, :], start=True, stop=True)
            last.then_inc(S["ssB_mm"], 1)

            pe.wait_ge(S["rB_ok"], 1)
            for h in range(H):
                g, lo = h // 2, 64 * (h % 2)
                out = ps[:, 4 + h, :]
                mm(out[:, 0:NP], ones, AA[:, h, 0:2, :].rearrange("p i t -> p (i t)"), start=True, stop=False)
                mm(out[:, P:NP], ones, AA[:, h, 2, :], start=False, stop=False)
                mm(out[:, NP:NT], ones[0:NS, :], AAs[:, h, :], start=False, stop=False)
                last = mm(out[:, NP:NT], ones[lo:lo + 64, :], qn[lo:lo + 64, g, :], start=False, stop=True)
            last.then_inc(S["denA_mm"], 1)

            pe.wait_ge(S["hA_sq"], 1)
            for h in range(H):
                last = mm(ps[:, h, 0:NT], ones, QB[:, h, :], start=True, stop=True)
            last.then_inc(S["ssA_mm"], 1)

            pe.wait_ge(S["kd_ok"], 1)
            pe.wait_ge(S["hA_ok"], 1)
            for i, (t0, r) in enumerate(TILES):
                for h in range(H):
                    last = nc.tensor.transpose(ps[0:r, 4 + i, h * P:(h + 1) * P], T[0][:, h, t0:t0 + r], ident)
            last.then_inc(S["kbt_mm"], 1)
            for i, (t0, r) in enumerate(TILES[0:2]):
                for g in range(2):
                    nc.tensor.transpose(ps[0:r, 7, (2 * i + g) * P:(2 * i + g + 1) * P], QK[:, 2 + g, t0:t0 + r], ident)
            pe.wait_ge(S["rA_ok"], 1)
            for g in range(2):
                last = nc.tensor.transpose(ps[0:NS, 0, g * P:(g + 1) * P], QK[:, 2 + g, NP:NT], ident)
            last.then_inc(S["kat_mm"], 1)

            def tokens_product(slot0, order, lhs, nk, done, waits):
                for n in range(nk):
                    k = order[n]
                    for w in waits.get(n, ()):
                        pe.wait_ge(*w)
                    slot_ready(slot0 + n)
                    w = ring[:, (slot0 + n) % RING, :]
                    for i, (t0, r) in enumerate(TILES):
                        for half in range(2):
                            last = mm(out_banks(i, half), lhs[:, k, t0:t0 + r], w[:, half * 512:(half + 1) * 512],
                                      start=n == 0, stop=n == nk - 1)
                    last.then_inc(S["slots_used"], 1)
                pe.wait_ge(S["slots_used"], slot0 + nk)
                pe.sem_inc(done, 1)

            tokens_product(OUT_SLOT0, OUT_ORDER, HT, KT, S["out_mm"],
                           {0: [(S["mixed"], 1), (S["kbt_ok"], 3), (S["kat_ok"], 3)], KT // 2: [(S["mixed"], 2)]})

            pe.wait_ge(S["old_ok"], 3)

            def state_done(last):
                last.then_inc(S["st_mm"], 1)

            def prompt_states():
                for h in range(H):
                    for i in range(2):
                        last = mm(ps[:, 5, h * DV:(h + 1) * DV], KBt[:, i, h * P:(h + 1) * P],
                                  V[:, i, 512 + h * DV:512 + (h + 1) * DV], start=i == 0, stop=i == 1)
                state_done(last)
                for h in range(H):
                    g, lo = h // 2, 64 * (h % 2)
                    for i in range(2):
                        mm(ps[lo:lo + 64, 6, g * DV:(g + 1) * DV], KAt[:, i, h * DKA:(h + 1) * DKA],
                           V[:, i, h * DV:(h + 1) * DV], start=i == 0, stop=i == 1)
                    for i in range(2):
                        mm(ps[lo:lo + 64, 6, 256 + g:257 + g], KAt[:, i, h * DKA:(h + 1) * DKA],
                           ones[:, 0:1], start=i == 0, stop=i == 1)
                mm(ps[:, 6, 320:320 + 2 * NSEQ], ident, n0[:, :, :].rearrange("p g b -> p (g b)"),
                   start=True, stop=False)
                for h in range(H):
                    g, lo = h // 2, 64 * (h % 2)
                    last = mm(ps[lo:lo + 64, 6, 320 + g * NSEQ:320 + (g + 1) * NSEQ],
                              KAt[0:NS, 2, h * DKA:(h + 1) * DKA], seq_of, start=False, stop=h >= 2)
                state_done(last)

            def sample_state(n):
                b0 = 5 if n % 2 == 0 else 0
                b1 = b0 + 1
                if n >= 2:
                    pe.wait_ge(S["st_ok"], 2 + n - 1)
                heads = [n] if n < H else [2 * (n - H), 2 * (n - H) + 1]
                for q, bank in enumerate((b0, b1)):
                    old = S0[:, 4 * q:4 * q + 4, n, :] if n < H else C0[:, 4 * q:4 * q + 4, n - H, :]
                    last = mm(ps[:, bank, :], ident, old, start=True, stop=False)
                    for h in heads:
                        vb = h if n < H else H + h
                        pe.wait_ge(S["vb_ok"], vb + 1)
                        if n < H:
                            last = mm(ps[:, bank, :], KBt[0:NS, 2, h * P:(h + 1) * P],
                                      VB[vb % len(VB)][0:NS, q * 512:(q + 1) * 512], start=False, stop=True)
                        else:
                            lo = 64 * (h % 2)
                            last = mm(ps[lo:lo + 64, bank, :], KAt[0:NS, 2, h * DKA:(h + 1) * DKA],
                                      VB[vb % len(VB)][0:NS, q * 512:(q + 1) * 512], start=False, stop=True)
                last.then_inc(S["vb_used"], len(heads))
                pe.wait_ge(S["vb_used"], (heads[-1] if n < H else H + heads[-1]) + 1)
                pe.sem_inc(S["st_mm"], 1)

            def route(i):
                t0, r = TILES[i]
                pe.wait_ge(S["x_norm"], 4 + i)
                pe.wait_ge(S["r1_ok"], 6)
                transpose_x(i, 6, 2)
                pe.wait_ge(S["xT_ok"], 8 + 2 * i)
                if i == 0:
                    pe.wait_ge(S["router_in"], 32)
                if i == 2:
                    pe.wait_ge(S["logits_ok"], 1)
                for k in range(KT):
                    last = mm(ps[0:r, (4, 7, 4)[i], 0:NE], xT[:, k, t0:t0 + r], w_r[:, k, :],
                              start=k == 0, stop=k == KT - 1)
                last.then_inc(S["router_mm"], 1)

            pe.sem_inc(S["xg_free"], 1)
            prompt_states()
            pe.wait_ge(S["st_ok"], 2)
            sample_state(0)
            route(0)
            sample_state(1)
            route(1)
            sample_state(2)
            route(2)

            pe.wait_ge(S["pick_ok"], 3)
            for i, (_, r) in enumerate(TILES):
                for j in range(i + 1):
                    rj = TILES[j][1]
                    mm(ps[:, 7, i * NE:(i + 1) * NE], (tri if j == i else ones)[0:rj, :], pick[0:rj, j, :],
                       start=j == 0, stop=j == i)
            for j, (_, r) in enumerate(TILES):
                last = mm(ps[:, 7, 3 * NE:4 * NE], ones[0:r, :], pick[0:r, j, :], start=j == 0, stop=j == 2)
            last.then_inc(S["rank_mm"], 1)
            sample_state(3)
            sample_state(4)
            sample_state(5)

            pe.wait_ge(S["st_ok"], 8)
            pe.wait_ge(S["p_in"], 48)
            for i, (t0, r) in enumerate(TILES):
                for g in range(2):
                    last = nc.tensor.transpose(ps[:, 5 + g, t0:t0 + r], p_in[0:r, i, g * P:(g + 1) * P], ident[0:r, 0:r])
            last.then_inc(S["pt_mm"], 1)

            def ple_products(b):
                pe.wait_ge(S["ple_w_in"], b * 32 + 32)
                for k in range(KT):
                    mm(ps[:, 5, 0:NT], ple_w[:, k, :], xT[:, k, :], start=k == 0, stop=k == KT - 1)
                for k in range(2):
                    last = mm(ps[:, 6, 0:NT], ple_w[:, KT + k, :], pT[:, k, :], start=k == 0, stop=k == 1)
                last.then_inc(S["ple_used"], 1)

            def ple_transposes(b):
                pe.wait_ge(S["ple_prod"], b + 1)
                pe.wait_ge(S["ple_added"], b + 1)
                pe.sem_inc(S["ple_seen"], 1)
                for i, (t0, r) in enumerate(TILES):
                    last = nc.tensor.transpose(ps[0:r, 2, i * P:(i + 1) * P], ple[:, t0:t0 + r], ident)
                last.then_inc(S["ple_t"], 1)

            def transpose_rows(b):
                pe.wait_ge(S["xg_full"], b * 16 + 16)
                pe.sem_inc(S["rows_seen"], 1)
                for k in range(KT):
                    last = nc.tensor.transpose(ps[:, 7, k * BLK:(k + 1) * BLK], x_g[0:BLK, k * P:(k + 1) * P],
                                               ident[0:BLK, 0:BLK])
                last.then_inc(S["xg_free"], 1)

            def expert_block(b, ahead, with_ple=False):
                pe.wait_ge(S["xTe_ok"], b + 1)
                pe.wait_ge(S["sel_ok"], b + 1)
                pe.wait_ge(S["gu_free"], b + 1)
                for w in range(2):
                    for half in range(2):
                        mm(ps[64 * half:64 * half + 64, w, :], sel[:, :], bias3[:, w, half * 512:(half + 1) * 512],
                           start=True, stop=False)
                for k in range(KT):
                    for w in range(2):
                        j = 2 * k + w
                        s = (PRE + j) % RING
                        pe.wait_ge(slot_full[s], b * (16 * PER // RING) + 16 * ((PRE + j) // RING + 1))
                        for half in range(2):
                            last = mm(ps[64 * half:64 * half + 64, w, :], xTe[:, k, :],
                                      ring[:, s, half * 512:(half + 1) * 512], start=False, stop=k == KT - 1)
                        last.then_inc(S["slots_used"], 1)
                if ahead:
                    transpose_rows(b + 1)
                if with_ple:
                    ple_products(b)
                pe.wait_ge(S["h_ok"], b + 1)
                for j in range(4):
                    last = nc.tensor.transpose(ps[:, 3, j * P:(j + 1) * P], h_s[:, j * P:(j + 1) * P], ident)
                last.then_inc(S["ht_mm"], 1)
                pe.wait_ge(S["y_free"], b + 1)
                for half in range(2):
                    mm(ps[64 * half:64 * half + 64, 4, :], sel[:, :], bias3[:, 2, half * 512:(half + 1) * 512],
                       start=True, stop=False)
                pe.wait_ge(S["hTe_ok"], b + 1)
                for k in range(KT):
                    j = 2 * KT + k
                    s = (PRE + j) % RING
                    pe.wait_ge(slot_full[s], b * (16 * PER // RING) + 16 * ((PRE + j) // RING + 1))
                    for half in range(2):
                        last = mm(ps[64 * half:64 * half + 64, 4, :],
                                  hTe[:, k % 4, (k // 4) * BLK:(k // 4 + 1) * BLK],
                                  ring[:, s, half * 512:(half + 1) * 512], start=False, stop=k == KT - 1)
                    last.then_inc(S["slots_used"], 1)
                if with_ple:
                    ple_transposes(b)

            pe.sem_inc(S["ple_used"], 1)
            pe.wait_ge(S["pT_ok"], 1)
            transpose_rows(0)
            with pe.Fori(0, PLE_BLOCKS) as b:
                expert_block(b, True, True)
            with pe.Fori(PLE_BLOCKS, NE - 1) as b:
                expert_block(b, True)
            expert_block(NE - 1, False)
            extra = pe.value_load(n_exti[0:1, 0:1], min_val=0, max_val=NEXTRA)
            with pe.If(extra > 0):
                with pe.Fori(0, NEXTRA) as j:
                    with pe.If(extra > j):
                        transpose_rows(j + NE)
                        expert_block(j + NE, False)

        @block.scalar
        def _(act):
            step = Steps(act, S["act_steps"])

            def f(out, in_, func, **kw):
                return nc.scalar.activation(out, in_, func, **kw)

            def norm_scale(n, r):
                act.wait_ge(S["ln_var"], n)
                step(f(mv[0:r, 2:3], mv[0:r, 1:2], ACT.Ln, bias=eps[0:r, 0:1]))
                f(mv[0:r, 3:4], mv[0:r, 2:3], ACT.Exp, scale=-0.5).then_inc(S["ln_rstd"], 1)

            def copy_xT(i, first, bank0):
                t0, r = TILES[i]
                for q in range(2):
                    act.wait_ge(S["xt_mm"], first + 2 * i + q + 1)
                    f(xT[:, 4 * q:4 * q + 4, t0:t0 + r], ps[:, bank0 + q, 0:4 * r].rearrange("p (k t) -> p k t", k=4),
                      ACT.Copy).then_inc(S["xT_ok"], 1)

            act.wait_ge(S["setup"], 1)
            for i in range(3):
                norm_scale(i + 1, TILES[i][1])
                if i:
                    copy_xT(i - 1, 0, 6)
            copy_xT(2, 0, 6)

            act.wait_ge(S["bias_ok"], 1)
            act.dma_start(y_rows[NE * BLK:, :].rearrange("r n -> (r n)").rearrange("(p q x) -> p q x", p=P, q=8),
                          view(AB, 0, ZROW).unsqueeze(1).to_broadcast([P, 8, ZROW])).then_inc(S["y_zero"], 16)

            def copy_values(base, off):
                for i, (_, r) in enumerate(TILES):
                    act.wait_ge(S["vt_mm"], base + i + 1)
                    f(V[0:r, i, off:off + 512], ps[0:r, 6 + (base + i) % 2, :], ACT.Copy).then_inc(S["v_ok"], 1)

            dest = [(G, j) for j in range(4)] + [(QB, j) for j in range(4)] + [(T[3], j) for j in range(4)] + \
                   [(None, 0)] + [(QK, j) for j in range(4)] + [(va_T, j) for j in range(4)] + \
                   [(GB, j) for j in range(4)] + [(OA, j) for j in range(4)]

            def decays(n):
                w = T[n % 2][:, :, :] if n < NLV - 1 else T[n % 2][:, :, 0:NP]
                act.wait_ge(S["sub_ok"], n)
                step(f(w, w, ACT.Abs))
                f(w, w, ACT.Exp, scale=-1.0).then_inc(S["w_ok"], 1)

            for c, (buf, j) in enumerate(dest):
                act.wait_ge(S["proj_mm"], c + 1)
                if c == 8:
                    act.wait_ge(S["bias_ok"], 1)
                if c == 25:
                    act.wait_ge(S["g_ok"], 1)
                    act.wait_ge(S["rows_ok"], 1)
                if buf is None:
                    step(f(rows[:, 0, :], ps[0:H, c % 3, 0:NT], ACT.Copy))
                    f(rows[:, 1, :], ps[32:32 + H, c % 3, 0:NT], ACT.Copy).then_inc(S["proj_ok"], 1)
                else:
                    f(buf[:, j, :], ps[:, c % 3, 0:NT], ACT.Copy,
                      scale=DKA ** -0.5 if buf is QK and j >= 2 else 1.0).then_inc(S["proj_ok"], 1)
                if c == 4:
                    act.wait_ge(S["z_ok"], 1)
                    f(T[0][:, :, :], G[:, :, :], ACT.Exp, scale=-1.0).then_inc(S["e_ok"], 1)
                    act.wait_ge(S["lb_max"], 1)
                    f(lb[:, 1, :], lb[:, 1, :], ACT.Exp).then_inc(S["lb_exp"], 1)
                if c == 7:
                    act.wait_ge(S["proj_ok"], 8)
                    f(T[2][:, :, :], QB[:, :, :], ACT.Exp, scale=-1.0).then_inc(S["eq_ok"], 1)
                if c == 8:
                    act.wait_ge(S["f_ok"], 1)
                    f(G[:, :, :], G[:, :, :], ACT.Ln).then_inc(S["lnf_ok"], 1)
                if c == 12:
                    decays(1)
                if c == 13:
                    copy_values(0, 512)
                    act.wait_ge(S["f_rows"], 1)
                    step(f(rows[:, 2, :], rows[:, 1, :], ACT.Abs))
                    step(f(rows[:, 2, :], rows[:, 2, :], ACT.Exp, scale=-1.0))
                    f(rows[:, 2, :], rows[:, 2, :], ACT.Ln, bias=eps[0:H, 2:3]).then_inc(S["sp_rows"], 1)
                if c == 14:
                    decays(2)
                if c == 16:
                    decays(3)
                    act.wait_ge(S["m_rows"], 1)
                    step(f(rows[:, 2, :], rows[:, 2, :], ACT.Exp))
                    step(f(r_int[:, :], r_int[:, :], ACT.Exp))
                    f(rows[:, 1, :], rows[:, 3, :], ACT.Exp, scale=-1.0).then_inc(S["rows_ok"], 1)
                if c == 18:
                    decays(4)
                if c == 20:
                    decays(5)
                if c == 21:
                    copy_values(3, 0)
                if 22 <= c < 26:
                    act.wait_ge(S["rbc_mm"], c - 21)
                    f(EM[:, c - 22, :], ps[:, 7, 0:NT], ACT.Copy).then_inc(S["em_ok"], 1)
                if c == 22:
                    decays(6)
                if c == 24:
                    decays(7)
                if c == 26:
                    decays(8)
                    act.wait_ge(S["d_ok"], H)
                    step(f(AA[:, :, :, :], AA[:, :, :, :], ACT.Exp))
                    f(AAs[:, :, :], AAs[:, :, :], ACT.Exp).then_inc(S["d_exp"], 1)
                    step(f(qg[:, :, :], G[:, :, NP:NT], ACT.Exp))
                    f(decB[:, :, :], G[:, :, NP + TS - 1:NT:TS], ACT.Exp).then_inc(S["gexp"], 1)

            act.wait_ge(S["proj_ok"], NPROJ)
            act.wait_ge(S["lvl_ok"], NLV)
            step(f(T[2][:, :, :], GB[:, :, :], ACT.Exp, scale=-1.0))
            f(T[3][:, :, :], OA[:, :, :], ACT.Exp, scale=-1.0).then_inc(S["gates_exp"], 1)
            act.wait_ge(S["oB_mm"], 1)
            step(f(T[0][:, :, :], ps[:, 4:8, 0:NT], ACT.Copy))
            f(T[1][:, :, :], T[0][:, :, :], ACT.Square).then_inc(S["oB_sq"], 1)
            act.wait_ge(S["ssB_mm"], 1)
            step(f(T[1][:, :, :], ps[:, 4:8, 0:NT], ACT.Ln, scale=1.0 / DV, bias=eps[:, 1:2]))
            f(T[1][:, :, :], T[1][:, :, :], ACT.Exp, scale=-0.5).then_inc(S["rB_ok"], 1)
            act.wait_ge(S["denA_mm"], 1)
            f(QB[:, :, :], ps[:, 4:8, 0:NT], ACT.Abs).then_inc(S["den_ok"], 1)
            act.wait_ge(S["mixed"], 1)
            for h in range(H):
                f(T[0][:, h, 0:NP], G[:, h, 0:NP], ACT.Exp, scale=-1.0, bias=G[:, h, NP - 1:NP]).then_inc(S["kd_exp"], 1)
            act.wait_ge(S["kd_sub"], 1)
            f(T[0][:, :, NP:NT], T[0][:, :, NP:NT], ACT.Exp).then_inc(S["kd_exp"], 1)
            act.wait_ge(S["hA_ok"], 1)
            f(QB[:, :, :], EM[:, :, :], ACT.Square).then_inc(S["hA_sq"], 1)
            act.wait_ge(S["ssA_mm"], 1)
            step(f(QB[:, :, :], ps[:, 0:4, 0:NT], ACT.Ln, scale=1.0 / DV, bias=eps[:, 1:2]))
            f(QB[:, :, :], QB[:, :, :], ACT.Exp, scale=-0.5).then_inc(S["rA_ok"], 1)
            act.wait_ge(S["kbt_mm"], 1)
            for i, (_, r) in enumerate(TILES):
                f(KBt[0:r, i, :], ps[0:r, 4 + i, :], ACT.Copy).then_inc(S["kbt_ok"], 1)

            def state_out(n):
                act.wait_ge(S["st_mm"], n + 1)
                if n == 0:
                    f(sp_s, ps[:, 5, :], ACT.Copy).then_inc(S["st_ok"], 1)
                elif n == 1:
                    step(f(cp_s, ps[:, 6, 0:256], ACT.Copy))
                    step(f(np_s[:, 0:2], ps[:, 6, 256:258], ACT.Copy))
                    f(np_s[:, 2:2 + 2 * NSEQ], ps[:, 6, 320:320 + 2 * NSEQ], ACT.Copy).then_inc(S["st_ok"], 1)
                else:
                    m = n - 2
                    b0 = 5 if m % 2 == 0 else 0
                    dst = S0[:, :, m, :] if m < H else C0[:, :, m - H, :]
                    f(dst, ps[:, b0:b0 + 2, :].rearrange("p q (b v) -> p (q b) v", b=4), ACT.Copy).then_inc(S["st_ok"], 1)

            def store_x(i):
                _, r = TILES[i]
                act.wait_ge(S["x_norm"], 4 + i)
                act.dma_start(x_rows[TILES[i][0]:TILES[i][0] + r, :], xs[0:r, i, :]).then_inc(S["x1_rows"], 16)

            def after_norm(i):
                store_x(i)
                copy_xT(i, 6, 2)

            def gates(i):
                r = TILES[i][1]
                act.wait_ge(S["top_ok"], i + 1)
                f(gate[0:r, i, :], top_v[0:r, i, 0:TOPK], ACT.Exp, bias=neg_v[0:r, i:i + 1],
                  accum_out=gsum[0:r, i:i + 1]).then_inc(S["gate_exp"], 1)

            norm_scale(4, P)
            state_out(0)
            state_out(1)
            norm_scale(5, P)
            norm_scale(6, NS)
            after_norm(0)
            state_out(2)
            after_norm(1)
            state_out(3)
            after_norm(2)
            state_out(4)
            for i in range(3):
                gates(i)
            state_out(5)
            state_out(6)
            state_out(7)
            act.wait_ge(S["st_ok"], 8)
            act.wait_ge(S["m_rows"], 1)
            with nc.allow_non_contiguous_dma(reason="small states laid out by partition"):
                act.dma_start(o[5][0, 0].rearrange("h d v -> d h v"), sp_s.rearrange("p (h v) -> p h v", h=H)).then_inc(S["st_out"], 16)
                for h in range(H):
                    g, lo = h // 2, 64 * (h % 2)
                    act.dma_start(o[2][0, 0, h], cp_s[lo:lo + 64, g * DV:(g + 1) * DV]).then_inc(S["st_out"], 16)
                    act.dma_start(o[3][0, 0, h:h + 1].rearrange("o d -> d o"), np_s[lo:lo + 64, g:g + 1]).then_inc(S["st_out"], 16)
                    act.dma_start(o[6][0, :, h].rearrange("b d v -> d b v"), C0[lo:lo + 64, :, g, :]).then_inc(S["st_out"], 16)
                    act.dma_start(o[7][0, :, h].rearrange("b d -> d b"),
                                  np_s[lo:lo + 64, 2 + g * NSEQ:2 + (g + 1) * NSEQ]).then_inc(S["st_out"], 16)
                act.dma_start(o[4][0].rearrange("b h -> h b"), rows[:, 3, NP - 1:NP]).then_inc(S["st_out"], 16)
                act.dma_start(o[8][0].rearrange("b h -> h b"), rows[:, 3, NP + TS - 1:NT:TS]).then_inc(S["st_out"], 16)
                act.dma_start(o[9][0].rearrange("b h d v -> d (b h) v"),
                              S0[:, :, :, :].rearrange("p b h v -> p (b h) v")).then_inc(S["st_out"], 16)

            act.wait_ge(S["pt_mm"], 1)
            f(pT[:, :, :], ps[:, 5:7, 0:NT], ACT.Copy).then_inc(S["pT_ok"], 1)

            def copy_rows(b):
                act.wait_ge(S["xg_free"], b + 2)
                f(xTe[:, :, :], ps[:, 7, :].rearrange("p (k s) -> p k s", k=KT), ACT.Copy).then_inc(S["xTe_ok"], 1)

            def expert_block(b, ahead, with_ple=False):
                act.wait_ge(S["g_ready"], b + 1)
                f(sg_s, g_s, ACT.Sigmoid, scale=SWIGLU_ALPHA).then_inc(S["sg_ok"], 1)
                if ahead:
                    copy_rows(b + 1)
                act.wait_ge(S["ht_mm"], b + 1)
                f(hTe[:, :, :], ps[:, 3, :].rearrange("p (j s) -> p j s", j=4), ACT.Copy).then_inc(S["hTe_ok"], 1)
                if with_ple:
                    act.wait_ge(S["ple_used"], b + 2)
                    f(ple, ps[:, 5, 0:NT], ACT.Sigmoid).then_inc(S["ple_sig"], 1)
                act.wait_ge(S["slots_used"], b * PER + (PRE + PER))
                act.wait_ge(S["y_stored"], b * 32 + 32)
                f(y_s, ps[:, 4, :], ACT.Copy).then_inc(S["y_free"], 1)
                act.wait_ge(S["y_free"], b + 2)
                for half in range(2):
                    act.dma_start(y_rows[bass.ds(b * BLK, BLK), half * 512:(half + 1) * 512],
                                  y_s[64 * half:64 * half + 64, :]).then_inc(S["y_stored"], 16)

            act.sem_inc(S["y_free"], 1)
            act.sem_inc(S["y_stored"], 32)
            copy_rows(0)
            with act.Fori(0, PLE_BLOCKS) as b:
                expert_block(b, True, True)
            with act.Fori(PLE_BLOCKS, NE - 1) as b:
                expert_block(b, True)
            expert_block(NE - 1, False)
            extra = act.value_load(n_exti[0:1, 0:1], min_val=0, max_val=NEXTRA)
            with act.If(extra > 0):
                with act.Fori(0, NEXTRA) as j:
                    with act.If(extra > j):
                        copy_rows(j + NE)
                        expert_block(j + NE, False)
            act.wait_ge(S["y_stored"], extra * 32 + (NE + 1) * 32)
            act.sem_inc(S["y_done"], 1)
            act.wait_ge(S["st_out"], 16 * 20)
            for i in range(3):
                norm_scale(7 + i, TILES[i][1])

        @block.vector
        def _(dve):
            step = Steps(dve, S["dve_steps"])
            tt, ts, stt = nc.vector.tensor_tensor, nc.vector.tensor_scalar, nc.vector.scalar_tensor_tensor

            step(nc.vector.memset(eps[:, 0:1], LN_EPS))
            step(nc.vector.memset(eps[:, 1:2], NORM_EPS))
            nc.vector.memset(eps[:, 2:3], 1.0).then_inc(S["setup"], 1)

            def norm(i, n, done):
                r = TILES[i][1]
                x = xs[0:r, i, :]
                for q in range(2):
                    step(nc.vector.bn_stats(lns[0:r, q, :], x[:, q * 512:(q + 1) * 512]))
                if n > 1:
                    dve.wait_ge(S["ln_rstd"], n - 1)
                nc.vector.bn_aggr(mv[0:r, 0:2], lns[0:r, :, :].rearrange("p q s -> p (q s)")).then_inc(S["ln_var"], 1)
                dve.wait_ge(S["ln_var"], n)
                step(stt(x, x, mv[0:r, 0:1], ln_g[0:r, :], ALU.subtract, ALU.mult))
                dve.wait_ge(S["ln_rstd"], n)
                stt(x, x, mv[0:r, 3:4], ln_b[0:r, :], ALU.mult, ALU.add).then_inc(S["x_norm"], 1)
                dve.wait_ge(S["x_norm"], n)

            for i in range(3):
                dve.wait_ge(S[f"x_in{i}"], 16)
                if i == 0:
                    dve.wait_ge(S["ln1_in"], 32)
                norm(i, i + 1, None)

            step(nc.vector.memset(flat(reset), 1.0))
            step(nc.vector.memset(reset[:, :, 0:1], 0.0))
            step(nc.vector.memset(reset[:, :, NP:NT:TS], 0.0))
            step(nc.vector.memset(oneh[:, :, :, :], 0.0))
            step(nc.vector.memset(AB[:, :, :, :], 0.0))
            step(nc.vector.memset(ABs[:, :, :], 0.0))
            step(nc.vector.memset(m0[:, 0:1], 0.0))
            dve.wait_ge(S["mask_in"], 16)
            step(nc.vector.tensor_copy(masks[:, :], flat(T[3])))
            dve.wait_ge(S["bias_in"], 48)
            for n in range(3):
                b, part = view(T[n], 0, D)[0:NE, :], view(T[3], 0, D)[0:NE, :]
                step(nc.vector.tensor_copy(bias3[0:NE, n, :], b))
                step(tt(part, b, bias3[0:NE, n, :], ALU.subtract))
                step(nc.vector.tensor_copy(sel2[0:NE, :], part))
                step(nc.vector.tensor_copy(bias3[NE:2 * NE, n, :], sel2[0:NE, :]))
                step(tt(part, part, sel2[0:NE, :], ALU.subtract))
                step(nc.vector.tensor_copy(bias3[2 * NE:3 * NE, n, :], part))
            dve.sem_inc(S["bias_ok"], 1)

            dve.wait_ge(S["vec_in"], 16 * 7)
            tt(lb[:, 1, :], lb[:, 0, :], lb[:, 0, :], ALU.subtract).then_inc(S["lb_max"], 1)
            dve.wait_ge(S["proj_ok"], 4)
            ts(G[:, :, :], G[:, :, :], -43.5, None, ALU.max).then_inc(S["z_ok"], 1)
            dve.wait_ge(S["lb_exp"], 1)
            step(nc.vector.reciprocal(lb[:, 2, :], lb[:, 1, :]))
            step(tt(lb[:, 2, :], lb[:, 1, :], lb[:, 2, :], ALU.mult))
            step(tt(lb[:, 3, :], lb[:, 2, :], lb[:, 2, :], ALU.subtract))
            step(ts(lb[:, 4, :], lb[:, 3, :], -1.0, 1.0, ALU.mult, ALU.add))
            step(ts(lb[:, 5, :], lb[:, 3, :], LB_FLOOR, None, ALU.max))
            dve.wait_ge(S["e_ok"], 1)
            step(ts(T[1][:, :, :], T[0][:, :, :], 1.0, None, ALU.add))
            step(nc.vector.reciprocal(T[1][:, :, :], T[1][:, :, :]))
            for h in range(H):
                step(ts(G[:, h, :], T[1][:, h, :], lb[:, 4, h:h + 1], lb[:, 5, h:h + 1], ALU.mult, ALU.add))
            dve.sem_inc(S["f_ok"], 1)
            for h in range(H):
                step(stt(KB[:, h, :], T[0][:, h, :], lb[:, 4, h:h + 1], T[1][:, h, :], ALU.mult, ALU.mult))
            dve.wait_ge(S["lnf_ok"], 1)
            nc.vector.tensor_tensor_scan(flat(G), flat(reset), flat(G), 0.0, ALU.mult, ALU.add).then_inc(S["g_ok"], 1)
            dve.wait_ge(S["g_ok"], 1)
            dve.wait_ge(S["eq_ok"], 1)
            step(ts(T[2][:, :, :], T[2][:, :, :], 1.0, None, ALU.add))
            step(nc.vector.reciprocal(T[2][:, :, :], T[2][:, :, :]))
            tt(QB[:, :, :], QB[:, :, :], T[2][:, :, :], ALU.mult).then_inc(S["mix_ok"], 1)
            dve.wait_ge(S["mix_ok"], 1)

            def sub(n):
                if n < NLV - 1:
                    half = 1 << (n - 1)
                    if half <= 16:
                        g = flat(G).rearrange("p (b m) -> p b m", m=2 * half)
                        w = flat(T[n % 2]).rearrange("p (b m) -> p b m", m=2 * half)
                        nb = H * NT // (2 * half)
                        tt(w, g, g[:, :, half - 1:half].to_broadcast([P, nb, 2 * half]),
                           ALU.subtract).then_inc(S["sub_ok"], 1)
                    else:
                        nb = NP // (2 * half)
                        g = G[:, :, 0:NP].rearrange("p h (b m) -> p h b m", m=2 * half)
                        w = T[n % 2][:, :, 0:NP].rearrange("p h (b m) -> p h b m", m=2 * half)
                        step(nc.vector.memset(T[n % 2][:, :, NP:NT], 0.0))
                        tt(w, g, g[:, :, :, half - 1:half].to_broadcast([P, H, nb, 2 * half]),
                           ALU.subtract).then_inc(S["sub_ok"], 1)
                else:
                    tt(T[n % 2][:, :, 0:NP], G[:, :, 0:NP], G[:, :, P - 1:P].to_broadcast([P, H, NP]),
                       ALU.subtract).then_inc(S["sub_ok"], 1)

            def mix(n):
                w, x = T[n % 2], T[2 + n % 2]
                dve.wait_ge(S["w_ok"], n)
                if n >= 3:
                    dve.wait_ge(S["lvl_mm"], n - 1)
                if n == 1:
                    dve.wait_ge(S["vt_mm"], 3)
                half = 1 << (n - 1)
                if half <= 16:
                    def parts(b):
                        return flat(b).rearrange("p (b m) -> p b m", m=2 * half)
                    lo, hi = (slice(None), slice(None), slice(0, half)), (slice(None), slice(None), slice(half, 2 * half))
                else:
                    def parts(b):
                        return b[:, :, 0:NP].rearrange("p h (b m) -> p h b m", m=2 * half)
                    lo = (slice(None),) * 3 + (slice(0, half),)
                    hi = (slice(None),) * 3 + (slice(half, 2 * half),)
                step(tt(parts(x)[lo], parts(KB)[lo], parts(w)[lo], ALU.mult))
                tt(parts(x)[hi], parts(QB)[hi], parts(w)[hi], ALU.mult).then_inc(S["mix_ok"], 1)
                dve.wait_ge(S["mix_ok"], n + 1)

            def take(n):
                dve.wait_ge(S["lvl_mm"], n + 1)
                if n == 0:
                    dve.wait_ge(S["y_zero"], 16)
                if n < NLV - 1:
                    if n <= 2:
                        step(nc.vector.copy_predicated(ABs[:, :, :], mask(n)[0:NS, 0:NS].unsqueeze(1).to_broadcast([NS, H, NS]),
                                                       ps[0:NS, 5, 0:H * NS].rearrange("p (h t) -> p h t", h=H)))
                    for q in range(2):
                        last = nc.vector.copy_predicated(
                            AB[:, 2 * q:2 * q + 2, 0:3:2, :],
                            mask(n).unsqueeze(1).unsqueeze(1).to_broadcast([P, 2, 2, P]),
                            ps[:, 3 + q, :].rearrange("p (h i t) -> p h i t", h=2, i=2))
                        if q == 0:
                            step(last)
                else:
                    last = nc.vector.tensor_copy(AB[:, :, 1, :], ps[:, 3, :].rearrange("p (h t) -> p h t", h=H))
                last.then_inc(S["lvl_ok"], 1)
                dve.wait_ge(S["lvl_ok"], n + 1)

            def gate_rows():
                fl, ir, w, m, b, bm = (rows[:, q, :] for q in (1, 0, 2, 3, 4, 5))
                st = rows[:, :, 0:NT]
                dve.wait_ge(S["proj_ok"], 13)
                step(ts(ir, ir, r_bias[:, 0:1], None, ALU.add))
                ts(fl, fl, r_bias[:, 1:2], None, ALU.add).then_inc(S["f_rows"], 1)

            def gate_rows2():
                fl, ir, w, m, b, bm = (rows[:, q, :] for q in (1, 0, 2, 3, 4, 5))
                dve.wait_ge(S["sp_rows"], 1)
                step(stt(fl, fl, 0.0, w, ALU.min, ALU.subtract))
                step(nc.vector.tensor_tensor_scan(b, reset[0:H, 0, :], fl, 0.0, ALU.mult, ALU.add))
                step(nc.vector.tensor_copy(w, ir))
                starts = ((slice(0, 1), slice(0, 1)), (slice(NP, NT, TS), slice(1, 1 + NSEQ)))
                for src, dst in starts:
                    step(tt(r_start[:, dst], fl[:, src], m0[:, dst], ALU.add))
                    step(tt(w[:, src], w[:, src], r_start[:, dst], ALU.max))
                    step(nc.vector.memset(fl[:, src], -1.0e30))
                step(nc.vector.tensor_tensor_scan(m, fl, w, -1.0e30, ALU.add, ALU.max))
                step(tt(bm, b, m, ALU.subtract))
                step(tt(ir, ir, b, ALU.subtract))
                step(tt(w[:, 0:NP], ir[:, 0:NP], bm[:, NP - 1:NP].to_broadcast([H, NP]), ALU.add))
                ws, bs, irs = (q[:, NP:NT].rearrange("p (b t) -> p b t", b=NSEQ) for q in (w, bm, ir))
                step(tt(ws, irs, bs[:, :, TS - 1:TS].to_broadcast([H, NSEQ, TS]), ALU.add))
                mb = m0[:, 1:1 + NSEQ]
                step(tt(r_int[:, 0:NS].rearrange("p (b t) -> p b t", b=NSEQ), bs,
                        mb.unsqueeze(2).to_broadcast([H, NSEQ, TS]), ALU.add))
                tt(r_int[:, NS:NS + NSEQ], bm[:, NP + TS - 1:NT:TS], mb, ALU.add).then_inc(S["m_rows"], 1)

            def gate_cols():
                dve.wait_ge(S["rcol_mm"], 1)
                step(nc.vector.tensor_copy(cols[:, 0:2, :, :], ps[:, 5, 0:4 * H].rearrange("p (i q h) -> p i q h", i=2, q=2)))
                step(nc.vector.tensor_copy(cols[0:NS, 2, :, :], ps[0:NS, 5, 4 * H:6 * H].rearrange("p (q h) -> p q h", q=2)))
                step(nc.vector.tensor_copy(inter[:, :, :], ps[:, 5, 64:64 + 2 * (NS + NSEQ)].rearrange("p (g c) -> p g c", g=2)))
                dve.wait_ge(S["state_in"], 16 * 9)
                tt(qi[:, :, :], QK[:, 0:2, NP:NT], inter[:, :, 0:NS], ALU.mult).then_inc(S["inter_ok"], 1)
                dve.wait_ge(S["inter_ok"], 1)
                step(tt(qn[:, :, :].rearrange("p g (b t) -> p g b t", b=NSEQ),
                        qi[:, :, :].rearrange("p g (b t) -> p g b t", b=NSEQ),
                        n0[:, :, :].unsqueeze(3).to_broadcast([P, 2, NSEQ, TS]), ALU.mult))

            def score_decay(h):
                dve.wait_ge(S["rbc_mm"], h + 1)
                step(ts(AA[:, h, 0:2, :].rearrange("p i t -> p (i t)"), ps[:, 6, 0:NP], cols[:, 0, 0, h:h + 1], 0.0, ALU.add, ALU.min))
                step(ts(AA[:, h, 2, :], ps[:, 6, P:NP], cols[:, 1, 0, h:h + 1], 0.0, ALU.add, ALU.min))
                ts(AAs[:, h, :], ps[0:NS, 6, NP:NT], cols[0:NS, 2, 0, h:h + 1], 0.0, ALU.add, ALU.min).then_inc(S["d_ok"], 1)
                dve.wait_ge(S["d_ok"], h + 1)

            sub(1)
            sub(2)
            take(0)
            gate_rows()
            mix(1)
            gate_rows2()
            take(1)
            for n in range(2, NLV):
                if n < NLV - 1:
                    sub(n + 1)
                mix(n)
                if n == 4:
                    gate_cols()
                if n == 5:
                    dve.wait_ge(S["vt_mm"], 6)
                    score_decay(0)
                if n == 6:
                    score_decay(1)
                if n == 7:
                    score_decay(2)
                    score_decay(3)
                if n < NLV - 1:
                    take(n)
            dve.wait_ge(S["d_exp"], 1)
            step(tt(scores(AA).rearrange("p h i t -> p h i t"), scores(AA),
                    tri.unsqueeze(1).unsqueeze(1).to_broadcast([P, H, 2, P]), ALU.mult))
            step(tt(AAs[:, :, :], AAs[:, :, :],
                    mask(1 + len(LEVELS))[0:NS, 0:NS].unsqueeze(1).to_broadcast([NS, H, NS]), ALU.mult))
            dve.wait_ge(S["gexp"], 1)
            tt(qg[:, :, :], qg[:, :, :], QB[:, :, NP:NT], ALU.mult).then_inc(S["qg_ok"], 1)
            dve.sem_inc(S["decB_ok"], 1)
            take(NLV - 1)

            dve.wait_ge(S["qk_mm"], 1)
            step(tt(AA[:, :, :, :].rearrange("p h i t -> p h (i t)"), AA[:, :, :, :].rearrange("p h i t -> p h (i t)"),
                    ps[:, 0:H, 0:384], ALU.mult))
            tt(AAs[:, :, :], AAs[:, :, :], ps[0:NS, 0:H, 384:384 + NS], ALU.mult).then_inc(S["sA_ok"], 1)
            dve.wait_ge(S["gates_exp"], 1)
            step(ts(T[2][:, :, :], T[2][:, :, :], 1.0, None, ALU.add))
            step(nc.vector.reciprocal(T[2][:, :, :], T[2][:, :, :]))
            step(tt(GB[:, :, :], GB[:, :, :], T[2][:, :, :], ALU.mult))
            step(ts(T[3][:, :, :], T[3][:, :, :], 1.0, None, ALU.add))
            step(nc.vector.reciprocal(T[3][:, :, :], T[3][:, :, :]))
            dve.wait_ge(S["rB_ok"], 1)
            step(tt(T[0][:, :, :], T[0][:, :, :], T[1][:, :, :], ALU.mult))
            for h in range(H):
                last = stt(HT[:, H + h, :], T[0][:, h, :], gains[:, 1, h:h + 1], GB[:, h, :], ALU.mult, ALU.mult)
                if h < H - 1:
                    step(last)
            last.then_inc(S["mixed"], 1)
            dve.wait_ge(S["mixed"], 1)
            dve.wait_ge(S["den_ok"], 1)
            step(tt(QB[:, :, :], QB[:, :, :], EM[:, :, :], ALU.max))
            step(nc.vector.reciprocal(QB[:, :, :], QB[:, :, :]))
            tt(EM[:, :, :], QB[:, :, :], ps[:, 0:H, 0:NT], ALU.mult).then_inc(S["hA_ok"], 1)
            dve.wait_ge(S["hA_ok"], 1)
            gs = G[:, :, NP:NT].rearrange("p h (b t) -> p h b t", b=NSEQ)
            tt(T[0][:, :, NP:NT].rearrange("p h (b t) -> p h b t", b=NSEQ),
               gs[:, :, :, TS - 1:TS].to_broadcast([P, H, NSEQ, TS]), gs, ALU.subtract).then_inc(S["kd_sub"], 1)
            dve.wait_ge(S["kd_exp"], H + 1)
            tt(T[0][:, :, :], T[0][:, :, :], KB[:, :, :], ALU.mult).then_inc(S["kd_ok"], 1)
            dve.wait_ge(S["rA_ok"], 1)
            step(tt(EM[:, :, :], EM[:, :, :], QB[:, :, :], ALU.mult))
            for h in range(H):
                last = stt(HT[:, h, :], EM[:, h, :], gains[:, 0, h:h + 1], T[3][:, h, :], ALU.mult, ALU.mult)
                if h < H - 1:
                    step(last)
            last.then_inc(S["mixed"], 1)
            dve.wait_ge(S["kat_mm"], 1)
            for i, (_, r) in enumerate(TILES):
                src = ps[0:r, 7, i * 256:(i + 1) * 256] if i < 2 else ps[0:r, 0, 0:256]
                tt(KAt[0:r, i, :].rearrange("p (h d) -> p h d", h=H), src.rearrange("p (h d) -> p h d", h=H),
                   cols[0:r, i, 1, :].unsqueeze(2).to_broadcast([r, H, DKA]), ALU.mult).then_inc(S["kat_ok"], 1)

            dve.wait_ge(S["out_mm"], 1)
            dve.wait_ge(S["ln2_in"], 32)
            for i, (_, r) in enumerate(TILES):
                for half in range(2):
                    x = xs[0:r, i, half * 512:(half + 1) * 512]
                    stt(x, x, ALPHA, out_banks(i, half), ALU.mult, ALU.add).then_inc(S["r1_ok"], 1)
            dve.wait_ge(S["r1_ok"], 6)
            for i in range(3):
                norm(i, 4 + i, None)

            for i, (_, r) in enumerate(TILES):
                dve.wait_ge(S["router_mm"], i + 1)
                tt(logit[0:r, :], ps[0:r, (4, 7, 4)[i], 0:NE], br[0:r, :], ALU.add).then_inc(S["logits_ok"], 1)
                dve.wait_ge(S["logits_ok"], i + 1)
                step(nc.vector.max(top_v[0:r, i, :], logit[0:r, :]))
                step(nc.vector.max_index(top_i[0:r, i, :], top_v[0:r, i, :], logit[0:r, :]))
                ts(neg_v[0:r, i:i + 1], top_v[0:r, i, 0:1], -1.0, None, ALU.mult).then_inc(S["top_ok"], 1)
                step(nc.vector.tensor_copy(top_f[0:r, i, :], top_i[0:r, i, :]))
                step(tt(oneh[0:r, i, :, :], iota[0:r, :].unsqueeze(1).to_broadcast([r, TOPK, NE]),
                        top_f[0:r, i, 0:TOPK].unsqueeze(2).to_broadcast([r, TOPK, NE]), ALU.is_equal))
                nc.vector.tensor_reduce(pick[0:r, i, :], oneh[0:r, i, :, :].rearrange("p k e -> p e k"),
                                        axis=AX_X, op=ALU.add).then_inc(S["pick_ok"], 1)
            dve.wait_ge(S["rank_mm"], 1)
            step(ts(rank[:, :, :], ps[:, 7, 0:3 * NE].rearrange("p (i e) -> p i e", i=3), -1.0, None, ALU.add))
            cnt = ps[:, 7, 3 * NE:4 * NE]
            step(ts(ex[:, 0, :], cnt, float(CHUNKS[0]), None, ALU.is_gt))
            step(ts(rt[:, 0, :, :], rank[:, :, :], float(CHUNKS[0]), None, ALU.is_ge))
            for c in CHUNKS[1:]:
                step(stt(ex[:, 0, :], cnt, float(c), ex[:, 0, :], ALU.is_gt, ALU.add))
                step(stt(rt[:, 0, :, :], rank[:, :, :], float(c), rt[:, 0, :, :], ALU.is_ge, ALU.add))
            step(nc.vector.tensor_tensor_scan(ex[:, 1, :], ones[:, 0:NE], ex[:, 0, :], 0.0, ALU.mult, ALU.add))
            step(tt(ex[:, 2, :], ex[:, 1, :], ex[:, 0, :], ALU.subtract))
            step(stt(ex[:, 2, :], ex[:, 2, :], float(NE - 1), iota, ALU.add, ALU.subtract))
            def bc3(v):
                return v.unsqueeze(1).to_broadcast([P, 3, NE])
            step(tt(rt[:, 1, :, :], rt[:, 0, :, :], bc3(ex[:, 2, :]), ALU.add))
            step(stt(rt[:, 1, :, :], rt[:, 0, :, :], 0.0, rt[:, 1, :, :], ALU.is_gt, ALU.mult))
            step(tt(rt[:, 1, :, :], rt[:, 1, :, :], bc3(iota), ALU.add))
            step(tt(rt[:, 1, :, :], rt[:, 1, :, :], rt[:, 0, :, :], ALU.subtract))
            step(stt(rank[:, :, :], rt[:, 1, :, :], float(BLK), rank[:, :, :], ALU.mult, ALU.add))
            for i in range(3):
                sel4 = ext[:, 0:TOPK, :]
                step(tt(sel4, oneh[:, i, :, :], rank[:, i, :].unsqueeze(1).to_broadcast([P, TOPK, NE]), ALU.mult))
                step(nc.vector.tensor_reduce(pos[:, i, :], sel4, axis=AX_X, op=ALU.add))
            step(nc.vector.tensor_copy(pos_i[:, :, :], pos[:, :, :]))
            step(nc.vector.tensor_copy(blk_e[:, 0:NE], iota))
            step(tt(ext[:, :, :], ex[:, 1, :].unsqueeze(1).to_broadcast([P, NEXTRA, NE]),
                    iota[:, 0:NEXTRA].unsqueeze(2).to_broadcast([P, NEXTRA, NE]), ALU.is_le))
            step(nc.vector.tensor_reduce(blk_e[:, NE:NBLK], ext[:, :, :], axis=AX_X, op=ALU.add))
            step(nc.vector.tensor_copy(blk_ei[:, :], blk_e[:, :]))
            nc.vector.tensor_copy(n_exti[:, :], ex[:, 1, NE - 1:NE]).then_inc(S["pos_ok"], 1)
            dve.wait_ge(S["gate_exp"], 3)
            for i, (_, r) in enumerate(TILES):
                step(nc.vector.reciprocal(gsum[0:r, i:i + 1], gsum[0:r, i:i + 1]))
                step(ts(gate[0:r, i, :], gate[0:r, i, :], gsum[0:r, i:i + 1], None, ALU.mult))

            def selector(b):
                ts(sel[:, :], cf[0:3 * NE, CF_PMOD:CF_PMOD + BLK], blk_e[0:3 * NE, bass.ds(b, 1)], None,
                   ALU.is_equal).then_inc(S["sel_ok"], 1)

            def expert_block(b, ahead, with_ple=False):
                dve.wait_ge(S["slots_used"], b * PER + (PRE + 2 * KT))
                ts(g_s, ps[:, 0, :], LIMIT, None, ALU.min).then_inc(S["g_ready"], 1)
                ts(u_s, ps[:, 1, :], LIMIT, -LIMIT, ALU.min, ALU.max).then_inc(S["gu_free"], 1)
                dve.wait_ge(S["g_ready"], b + 1)
                dve.wait_ge(S["gu_free"], b + 2)
                stt(u_s, u_s, 1.0, g_s, ALU.add, ALU.mult).then_inc(S["ug_ok"], 1)
                dve.wait_ge(S["ug_ok"], b + 1)
                dve.wait_ge(S["sg_ok"], b + 1)
                tt(h_s, u_s, sg_s, ALU.mult).then_inc(S["h_ok"], 1)
                if ahead:
                    dve.wait_ge(S["slots_used"], b * PER + (PRE + 2 * KT + 1))
                    selector(b + 1)
                if with_ple:
                    dve.wait_ge(S["ple_sig"], b + 1)
                    tt(ple, ple, ps[:, 6, 0:NT], ALU.mult).then_inc(S["ple_prod"], 1)
                    dve.wait_ge(S["ple_t"], b + 1)
                    for i, (_, r) in enumerate(TILES):
                        x = xs[0:r, i, bass.ds(b * P, P)]
                        last = stt(x, x, ALPHA, ps[0:r, 2, i * P:(i + 1) * P], ALU.mult, ALU.add)
                    last.then_inc(S["ple_added"], 1)

            dve.wait_ge(S["x1_rows"], 48)
            dve.sem_inc(S["ple_added"], 1)
            dve.sem_inc(S["gu_free"], 1)
            selector(0)
            with dve.Fori(0, PLE_BLOCKS) as b:
                expert_block(b, True, True)
            with dve.Fori(PLE_BLOCKS, NE - 1) as b:
                expert_block(b, True)
            expert_block(NE - 1, False)
            extra = dve.value_load(n_exti[0:1, 0:1], min_val=0, max_val=NEXTRA)
            with dve.If(extra > 0):
                with dve.Fori(0, NEXTRA) as j:
                    with dve.If(extra > j):
                        dve.wait_ge(S["slots_used"], j * PER + (PRE + NE * PER))
                        selector(j + NE)
                        expert_block(j + NE, False)

            dve.wait_ge(S["ln3_in"], 32)
            for i, (_, r) in enumerate(TILES):
                dve.wait_ge(S[f"picked{i}"], 16 * TOPK)
                for k in range(TOPK):
                    step(stt(xs[0:r, i, :], ring[0:r, i * TOPK + k, :], gate[0:r, i, k:k + 1], xs[0:r, i, :],
                             ALU.mult, ALU.add))
                norm(i, 7 + i, None)


_INS = ["x_prompt", "x_sample", "state_mlstm_C", "state_mlstm_n", "state_mlstm_m", "state_hgrn_S", "p_prompt",
        "p_sample", "ln_in_g", "ln_in_b", "w_in", "mlstm_ig_bias", "mlstm_fg_bias", "mlstm_norm_g",
        "hgrn_lb_logits", "hgrn_norm_g", "w_out", "ln1_g", "ln1_b", "w_router", "b_router", "w_gate", "b_gate",
        "w_up", "b_up", "w_down", "b_down", "w_ple_gate", "w_ple_proj", "ln2_g", "ln2_b"]
_OUTS = [(1, 256, 1024), (8, 4, 1024), (1, 1, 4, 64, 128), (1, 1, 4, 64), (1, 1, 4), (1, 1, 4, 128, 128),
         (1, 8, 4, 64, 128), (1, 8, 4, 64), (1, 8, 4), (1, 8, 4, 128, 128)]


def kernel(**inputs):
    import numpy as _np
    import concourse.bacc as _bacc
    from concourse import mybir as _mybir
    from concourse.bass_utils import run_bass_kernel_spmd as _run

    nc = _bacc.Bacc("TRN2", target_bir_lowering=False, num_devices=1)
    arrays, aps = {}, {}
    given = [(n, inputs[n]) for n in _INS] + list(zip(("const_f", "const_m", "const_t"), constant_arrays()))
    for name, value in given:
        v = _np.ascontiguousarray(value)
        arrays[f"in_{name}"] = v
        aps[name] = nc.dram_tensor(f"in_{name}", v.shape, _mybir.dt.from_np(v.dtype), kind="ExternalInput").ap()
    outs = [nc.dram_tensor(f"out_{n}", shape, _mybir.dt.float32, kind="ExternalOutput").ap()
            for n, shape in enumerate(_OUTS)]
    trunk_step(nc, aps, outs)
    r = _run(nc, [arrays], core_ids=[0])
    return tuple(r.results[0][f"out_{n}"] for n in range(len(_OUTS)))
```

```python
from contextlib import ExitStack

import numpy as np

import concourse.bass as bass
from concourse import mybir

F32 = mybir.dt.float32
BF16 = mybir.dt.bfloat16
I32 = mybir.dt.int32
U32 = mybir.dt.uint32
U8 = mybir.dt.uint8
ALU = mybir.AluOpType
ACT = mybir.ActivationFunctionType
AX_X = mybir.AxisListType.X

P = 128
D = 1024
KT = D // P
NP, NSEQ, TS = 256, 8, 4
NS = NSEQ * TS
NT = NP + NS
TILES = [(0, P), (P, P), (NP, NS)]
H = 4
DKA, DV = 64, 128
NE, TOPK = 32, 4
DPLE = 256
BLK = 64
NEXTRA = (NT * TOPK - 1) // BLK
NBLK = NE + NEXTRA
CHUNKS = [BLK * c for c in range(1, -(-NT // BLK))]
ALPHA = 2.0 ** 0.25
LN_EPS, NORM_EPS, LB_FLOOR = 1e-5, 1e-6, 1e-20
HEAD_BLOCKS = 4
PLE_END = HEAD_BLOCKS + 2 * KT
CB_BANKS = (2, 6, 3, 2, 6)
CB_NEEDS = (0, 0, 0, 1, 2)
LIMIT, SWIGLU_ALPHA = 7.0, 1.702
LEVELS = [1, 2, 4, 8, 16, 32, 64]

RING = 12
W_GROUPS = [2056, 1544, 2568, 0, 512, 3080, 1024]
IF_COL = 1536
IN_SLOTS = 4 * len(W_GROUPS)
OUT_SLOT0 = IN_SLOTS
PRE = OUT_SLOT0 + KT
PER = 3 * KT

CF_IDENT, CF_ONES, CF_TRI, CF_HEAD, CF_PMOD, CF_IOTA, CF_SEQ = 0, 128, 256, 384, 896, 1024, 1088
CF_W = 1096


def constant_arrays():
    p = np.arange(P)[:, None]
    t = np.arange(P)[None, :]
    f = np.zeros((P, CF_W), np.float32)
    f[:, CF_IDENT:CF_IDENT + P] = p == t
    f[:, CF_ONES:CF_ONES + P] = 1.0
    f[:, CF_TRI:CF_TRI + P] = t >= p
    for h in range(H):
        f[h, CF_HEAD + h * P:CF_HEAD + (h + 1) * P] = 1.0
    f[:, CF_PMOD:CF_PMOD + BLK] = p % NE
    f[:, CF_IOTA:CF_IOTA + BLK] = np.arange(BLK)
    f[:, CF_SEQ:CF_SEQ + NSEQ] = (p // TS) == np.arange(NSEQ)
    m = np.zeros((P, 2 + len(LEVELS), P), np.float32)
    m[:, 0] = p == t
    for n, half in enumerate(LEVELS):
        m[:, 1 + n] = (p // (2 * half) == t // (2 * half)) & (p % (2 * half) < half) & (t % (2 * half) >= half)
    m[:, 1 + len(LEVELS)] = (t >= p) & (p // TS == t // TS)
    return f, m.reshape(P, -1)


class Steps:

    def __init__(self, eng, sem):
        self.eng, self.sem, self.n = eng, sem, 0

    def __call__(self, ins):
        self.n += 1
        ins.then_inc(self.sem, 1)
        self.eng.wait_ge(self.sem, self.n)


def trunk_step(nc, a, o):
    w_in = a["w_in"][0].rearrange("(kt p) n -> p kt n", p=P)
    w_out = a["w_out"][0].rearrange("(kt p) n -> kt p n", p=P)
    w_pg = a["w_ple_gate"][0].rearrange("(kt p) n -> p kt n", p=P)
    w_pp = a["w_ple_proj"][0].rearrange("(kt p) n -> p kt n", p=P)
    w_ex = [a[n].rearrange("l e (kt p) n -> (l e) kt p n", p=P) for n in ("w_gate", "w_up", "w_down")]
    x_src = [a["x_prompt"][0, 0:P, :], a["x_prompt"][0, P:NP, :], a["x_sample"].rearrange("b t d -> (b t) d")]
    p_src = [a["p_prompt"][0, 0, 0:P, :], a["p_prompt"][0, 0, P:NP, :],
             a["p_sample"].rearrange("l b t d -> (l b t) d")]
    y_dst = [o[0][0, 0:P, :], o[0][0, P:NP, :], o[1].rearrange("b t d -> (b t) d")]

    with ExitStack() as ctx:
        def sb(name, shape, dt=F32):
            return ctx.enter_context(nc.sbuf_tensor(name, shape, dt))

        class Semaphores(dict):

            def __missing__(self, name):
                self[name] = ctx.enter_context(nc.semaphore(name))
                return self[name]

        S = Semaphores()
        slot_full = [S[f"slot_full{n}"] for n in range(RING)]

        ring = sb("ring", [P, RING, D])
        xs = sb("xs", [P, 3, D])
        ln_g, ln_b = sb("ln_g", [P, D]), sb("ln_b", [P, D])
        xT = sb("xT", [P, KT, NT])
        HT = xT
        cf = sb("cf", [P, CF_W])
        masks = sb("masks", [P, (2 + len(LEVELS)) * P], U8)
        eps = sb("eps", [P, 4])
        lns = sb("lns", [P, 3, 2, 6])
        mv = sb("mv", [P, 3, 4])
        w_if = sb("w_if", [P, KT, 2 * H])
        w_r = sb("w_r", [P, KT, NE])
        br = sb("br", [P, NE])
        G = sb("G", [P, H, NT])
        KB, QB = sb("KB", [P, H, NT]), sb("QB", [P, H, NT])
        GB, OA = sb("GB", [P, H, NT]), sb("OA", [P, H, NT])
        QK = sb("QK", [P, 4, NT])
        T = [sb(f"T{n}", [P, H, NT]) for n in range(4)]
        V = sb("V", [P, 3, D])
        AB, ABs = sb("AB", [P, H, 3, P]), sb("ABs", [NS, H, NS])
        AA, AAs = sb("AA", [P, H, 3, P]), sb("AAs", [NS, H, NS])
        S0 = sb("S0", [P, NSEQ, H, DV])
        C0 = sb("C0", [P, NSEQ, 2, DV])
        n0 = sb("n0", [P, 2, NSEQ])
        EM = sb("EM", [P, H, NT])
        rows = sb("rows", [H, 6, NT])
        r_bias = sb("r_bias", [H, 2])
        m0 = sb("m0", [H, 1 + NSEQ])
        r_start = sb("r_start", [H, 1 + NSEQ])
        cols = sb("cols", [P, 3, 2, H])
        inter = sb("inter", [P, 2, NS + NSEQ])
        decB = sb("decB", [P, H, NSEQ])
        qg = sb("qg", [P, H, NS])
        qi = sb("qi", [P, 2, NS])
        qn = sb("qn", [P, 2, NS])
        qi2 = sb("qi2", [P, 2, NSEQ, 2, TS])
        r_int = sb("r_int", [H, NS + NSEQ])
        gains = sb("gains", [P, 2, H])
        lb = sb("lb", [P, 6, H])
        logit = sb("logit", [P, NE])
        top_v = sb("top_v", [P, 3, 8])
        top_i = sb("top_i", [P, 3, 8], U32)
        top_f = sb("top_f", [P, 3, 8])
        neg_v = sb("neg_v", [P, 3])
        gsum = sb("gsum", [P, 3])
        gate = sb("gate", [P, 3, TOPK])
        oneh = sb("oneh", [P, 3, TOPK, NE])
        pick = sb("pick", [P, 3, NE])
        ex = sb("ex", [P, 4, NE])
        row_of = sb("row_of", [P, 3, NE + 1])
        gate_of = sb("gate_of", [P, 3, NE + 1])
        OH = sb("OH", [P, 3, BLK], BF16)
        blk_e = sb("blk_e", [P, NBLK])
        blk_ei = sb("blk_ei", [P, NBLK], I32)
        ext = sb("ext", [P, NEXTRA, NE])
        n_exti = sb("n_exti", [P, 1], I32)
        bias3 = sb("bias3", [3 * NE, 3, D], BF16)
        sel = sb("sel", [3 * NE, BLK], BF16)
        sel2 = sb("sel2", [NE, D], BF16)

        def view(buf, start, size):
            flat = buf[:, :, :].rearrange("p a b -> p (a b)") if len(buf.shape) == 3 \
                else buf[:, :, :, :].rearrange("p a b c -> p (a b c)")
            return flat[:, start:start + size]

        reset = OA
        va_T = view(AA, 0, H * NT).rearrange("p (h t) -> p h t", h=H)
        VB = [view(b, 0, NSEQ * DV) for b in (T[1], T[2])]
        KBt = view(AB, 0, 3 * 512).rearrange("p (i n) -> p i n", i=3)
        KAt = view(AA, 0, 3 * 256).rearrange("p (i n) -> p i n", i=3)
        sp_s, cp_s, np_s = view(T[3], 0, 512), view(T[3], 512, 256), view(T[3], 768, 2 + 2 * NSEQ)
        p_in = view(T[1], 0, 3 * DPLE).rearrange("p (i d) -> p i d", i=3)
        pT = view(QK, 0, 2 * NT).rearrange("p (k t) -> p k t", k=2)
        ple_w = view(V, 0, 10 * P).rearrange("p (k n) -> p k n", k=10)
        ple = T[0][:, 0, :]
        split_tmp = view(OA, 0, D)
        xb = [view(b, off, 512).bitcast(BF16) for b, off in
              ((G, 0), (G, 512), (GB, 0), (GB, 512), (EM, 0), (EM, 512), (KB, 512), (T[0], 512), (QK, 2 * NT))]
        xTe = view(KB, 0, KT * BLK).rearrange("p (k s) -> p k s", k=KT)
        g_s, u_s = view(OA, 0, 512), view(OA, 512, 512)
        sg_s, h_s = view(T[3], 0, 512), view(T[3], 512, 512)
        hTe = view(QB, 0, 512).rearrange("p (j s) -> p j s", j=4)
        y_s = view(QB, 512, 512)
        GW = view(AA, 768, 3 * BLK).rearrange("p (i s) -> p i s", i=3)
        GT = view(AA, 1024, NT)

        ps = ctx.enter_context(nc.psum_tensor("ps", [P, 8, 512], F32))

        ident = cf[:, CF_IDENT:CF_IDENT + P]
        ones = cf[:, CF_ONES:CF_ONES + P]
        tri = cf[:, CF_TRI:CF_TRI + P]
        iota = cf[:, CF_IOTA:CF_IOTA + NE]
        seq_of = cf[0:NS, CF_SEQ:CF_SEQ + NSEQ]

        def head_row(h, n=P):
            return cf[0:H, CF_HEAD + h * P:CF_HEAD + h * P + n]

        def mask(n):
            return masks[:, n * P:(n + 1) * P]

        def scores(buf, part=P):
            return buf[0:part, :, 0:3:2, :]

        def flat(buf):
            return buf[:, :, :].rearrange("p h t -> p (h t)")

        def num_s(g):
            return ps[:, 2 * g, NP:NP + 2 * NS].rearrange("p (b q t) -> p b q t", b=NSEQ, q=2)

        def out_banks(i, half):
            r = TILES[i][1]
            if i < 2:
                return ps[0:r, 2 * i + half, :]
            return ps[64 * half:64 * half + r, 4, :]

        NLV = 2 + len(LEVELS)
        LVL_TILE = {12 + 2 * n: n for n in range(NLV)}
        NPROJ = 29
        rows_iota = cf[:, CF_IOTA:CF_IOTA + BLK]
        N_VB = 2 * H

        block = ctx.enter_context(nc.Block())

        @block.sync
        def _(sp):
            used = [0]
            for i, (_, r) in enumerate(TILES):
                sp.dma_start(xs[0:r, i, :], x_src[i]).then_inc(S[f"x_in{i}"], 16)
                if i == 0:
                    sp.dma_start(ln_g[:, :], a["ln_in_g"].partition_broadcast(P)).then_inc(S["ln1_in"], 16)
                    sp.dma_start(ln_b[:, :], a["ln_in_b"].partition_broadcast(P)).then_inc(S["ln1_in"], 16)
                    sp.dma_start(cf[:, :], a["const_f"]).then_inc(S["const_in"], 16)

            def ring_load(src, split):
                n, s = used[0], used[0] % RING
                if n >= RING:
                    sp.wait_ge(S["slots_used"], n - RING + 1)
                dst = ring[:, s, :].rearrange("p (k n) -> p k n", k=2) if split else ring[:, s, :]
                sp.dma_start(dst, src).then_inc(slot_full[s], 16)
                used[0] += 1

            for c0 in W_GROUPS:
                for q in range(4):
                    ring_load(w_in[:, 2 * q:2 * q + 2, c0:c0 + 512], True)
            for src in [w_out[k] for k in range(KT)]:
                ring_load(src, False)

            def expert_weights(b, e, tile=None):
                order = [(w, k) for k in range(KT) for w in (0, 1)] + [(2, k) for k in range(KT)]
                for j, (w, k) in enumerate(order):
                    if tile is not None and j == RING:
                        sp.wait_ge(S["ple_used"], tile + 1)
                        sp.dma_start(ple_w[:, 0:KT, :], w_pg[:, :, bass.ds(tile * P, P)]).then_inc(S["ple_w_in"], 16)
                        sp.dma_start(ple_w[:, KT:KT + 2, :], w_pp[:, :, bass.ds(tile * P, P)]).then_inc(S["ple_w_in"], 16)
                    s = (PRE + j) % RING
                    sp.wait_ge(S["slots_used"], b * PER + (PRE + j - RING + 1))
                    sp.dma_start(ring[:, s, :],
                                 w_ex[w][bass.ds(e, 1), k, :, :].rearrange("e p n -> p (e n)")
                                 ).then_inc(slot_full[s], 16)

            with sp.Fori(0, HEAD_BLOCKS) as b:
                expert_weights(b, b)
            with sp.Fori(0, KT) as c:
                expert_weights(c * 2 + HEAD_BLOCKS, c * 2 + HEAD_BLOCKS, c)
                expert_weights(c * 2 + (HEAD_BLOCKS + 1), c * 2 + (HEAD_BLOCKS + 1))
            with sp.Fori(PLE_END, NE) as b:
                expert_weights(b, b)
            sp.wait_ge(S["pos_ok"], 1)
            extra = sp.value_load(n_exti[0:1, 0:1], min_val=0, max_val=NEXTRA)
            with sp.If(extra > 0):
                with sp.Fori(0, NEXTRA) as j:
                    with sp.If(extra > j):
                        e = sp.value_load(blk_ei[0:1, bass.ds(j + NE, 1)], min_val=0, max_val=NE - 1)
                        expert_weights(j + NE, e)
            for i, (_, r) in enumerate(TILES):
                sp.wait_ge(S["x_norm"], 7 + i)
                sp.dma_start(y_dst[i], xs[0:r, i, :]).then_inc(S["y_out"], 16)
            sp.wait_ge(S["y_out"], 48)

        @block.gpsimd
        def _(pool):
            with nc.allow_non_contiguous_dma(reason="small vectors laid out by partition"):
                for n, name in enumerate(("b_gate", "b_up", "b_down")):
                    pool.dma_start(view(T[n], 0, D)[0:NE, :], a[name][0]).then_inc(S["bias_in"], 16)
                pool.dma_start(flat(T[3]), a["const_m"]).then_inc(S["mask_in"], 16)
                pool.dma_start(lb[:, 0, :], a["hgrn_lb_logits"][0].rearrange("(h d) -> d h", d=P)).then_inc(S["vec_in"], 16)
                pool.dma_start(gains[:, 0, :], a["mlstm_norm_g"][0].rearrange("(h d) -> d h", d=P)).then_inc(S["vec_in"], 16)
                pool.dma_start(gains[:, 1, :], a["hgrn_norm_g"][0].rearrange("(h d) -> d h", d=P)).then_inc(S["vec_in"], 16)
                pool.dma_start(r_bias[:, 0:1], a["mlstm_ig_bias"].rearrange("l h -> h l")).then_inc(S["vec_in"], 16)
                pool.dma_start(r_bias[:, 1:2], a["mlstm_fg_bias"].rearrange("l h -> h l")).then_inc(S["vec_in"], 16)
                pool.dma_start(m0[:, 1:1 + NSEQ], a["state_mlstm_m"][0].rearrange("b h -> h b")).then_inc(S["vec_in"], 16)
                pool.dma_start(w_if[:, :, :], w_in[:, :, IF_COL:IF_COL + 2 * H]).then_inc(S["if_in"], 16)
                pool.dma_start(S0[:, :, :, :].rearrange("p b h v -> p (b h) v"),
                               a["state_hgrn_S"][0].rearrange("b h d v -> d (b h) v")).then_inc(S["state_in"], 16)
                for h in range(H):
                    g, hh = h // 2, h % 2
                    pool.dma_start(C0[64 * hh:64 * hh + 64, :, g, :],
                                   a["state_mlstm_C"][0, :, h].rearrange("b d v -> d b v")).then_inc(S["state_in"], 16)
                    pool.dma_start(n0[64 * hh:64 * hh + 64, g, :],
                                   a["state_mlstm_n"][0, :, h].rearrange("b d -> d b")).then_inc(S["state_in"], 16)
                pool.dma_start(w_r[:, :, :], a["w_router"][0].rearrange("(kt p) n -> p kt n", p=P)).then_inc(S["router_in"], 16)
                pool.dma_start(br[:, :], a["b_router"][0].partition_broadcast(P)).then_inc(S["router_in"], 16)
                pool.wait_ge(S["x_norm"], 3)
                pool.dma_start(ln_g[:, :], a["ln1_g"][0].partition_broadcast(P)).then_inc(S["ln2_in"], 16)
                pool.dma_start(ln_b[:, :], a["ln1_b"][0].partition_broadcast(P)).then_inc(S["ln2_in"], 16)

            pool.wait_ge(S["decB_ok"], 1)
            pool.wait_ge(S["inter_ok"], 1)
            pool.wait_ge(S["hA_ok"], 1)
            pool.wait_ge(S["oB_mm"], 1)
            nc.gpsimd.tensor_tensor(S0[:, :, :, :], S0[:, :, :, :],
                                    decB[:, :, :].rearrange("p h b -> p b h").unsqueeze(3).to_broadcast([P, NSEQ, H, DV]),
                                    ALU.mult).then_inc(S["old_ok"], 1)
            dec_a = inter[:, :, NS:NS + NSEQ]
            nc.gpsimd.tensor_tensor(C0[:, :, :, :], C0[:, :, :, :],
                                    dec_a.rearrange("p g b -> p b g").unsqueeze(3).to_broadcast([P, NSEQ, 2, DV]),
                                    ALU.mult).then_inc(S["old_ok"], 1)
            nc.gpsimd.tensor_tensor(n0[:, :, :], n0[:, :, :], dec_a, ALU.mult).then_inc(S["old_ok"], 1)
            pool.wait_ge(S["mixed"], 2)
            for n in range(N_VB):
                if n >= len(VB):
                    pool.wait_ge(S["vb_used"], n - len(VB) + 1)
                off = 512 + n * DV if n < H else (n - H) * DV
                nc.gpsimd.tensor_tensor(VB[n % len(VB)][0:NS, :].rearrange("p (b v) -> p b v", b=NSEQ),
                                        V[0:NS, 2, off:off + DV].unsqueeze(1).to_broadcast([NS, NSEQ, DV]),
                                        seq_of.unsqueeze(2).to_broadcast([NS, NSEQ, DV]),
                                        ALU.mult).then_inc(S["vb_ok"], 1)
                if n == 1:
                    pool.wait_ge(S["x_norm"], 6)
                    pool.dma_start(ln_g[:, :], a["ln2_g"][0].partition_broadcast(P)).then_inc(S["ln3_in"], 16)
                    pool.dma_start(ln_b[:, :], a["ln2_b"][0].partition_broadcast(P)).then_inc(S["ln3_in"], 16)
            pool.wait_ge(S["vb_used"], N_VB)
            for i, (_, r) in enumerate(TILES):
                pool.dma_start(p_in[0:r, i, :], p_src[i]).then_inc(S["p_in"], 16)

        @block.tensor
        def _(pe):
            mm = nc.tensor.matmul

            def slot_ready(n):
                pe.wait_ge(slot_full[n % RING], 16 * (n // RING + 1))

            pe.wait_ge(S["const_in"], 16)

            def transpose_x(i, first, bank0):
                r = TILES[i][1]
                for q in range(2):
                    n = first + 2 * i + q
                    if n >= 2:
                        pe.wait_ge(S["xT_ok"], n - 1)
                    dst = ps[:, bank0 + q, 0:4 * r].rearrange("p (k t) -> p k t", k=4)
                    for k in range(4):
                        c = 4 * q + k
                        last = nc.tensor.transpose(dst[:, k, :], xs[0:r, i, c * P:(c + 1) * P], ident[0:r, 0:r])
                    last.then_inc(S["xt_mm"], 1)

            for i in range(3):
                pe.wait_ge(S["x_norm"], i + 1)
                transpose_x(i, 0, 6)
            pe.wait_ge(S["xT_ok"], 6)

            def project(c, group, j):
                bank = c % 3
                if c >= 3:
                    pe.wait_ge(S["proj_ok"], c - 2)
                if group is None:
                    pe.wait_ge(S["if_in"], 16)
                    for k in range(KT):
                        mm(ps[0:H, bank, 0:NT], w_if[:, k, 0:H], xT[:, k, :], start=k == 0, stop=k == KT - 1)
                        last = mm(ps[32:32 + H, bank, 0:NT], w_if[:, k, H:2 * H], xT[:, k, :],
                                  start=k == 0, stop=k == KT - 1)
                    last.then_inc(S["proj_mm"], 1)
                    return
                for k in range(KT):
                    n = 4 * group + k // 2
                    if j == 0 and k % 2 == 0:
                        slot_ready(n)
                    w = ring[:, n % RING, (k % 2) * 512 + j * P:(k % 2) * 512 + (j + 1) * P]
                    last = mm(ps[:, bank, 0:NT], w, xT[:, k, :], start=k == 0, stop=k == KT - 1)
                    if k == KT - 1:
                        last.then_inc(S["proj_mm"], 1)
                    elif j == 3 and k % 2 == 1:
                        last.then_inc(S["slots_used"], 1)
                if j == 3:
                    pe.wait_ge(S["proj_mm"], c + 1)
                    pe.sem_inc(S["slots_used"], 1)

            def level(n):
                half = 1 << (n - 1) if n else 0
                src_k, src_q = (KB, QB) if n == 0 else (T[2 + n % 2], T[2 + n % 2])
                pe.wait_ge(S["mix_ok"], n + 1)
                if n:
                    pe.wait_ge(S["lvl_ok"], n)
                for h in range(H):
                    if n < NLV - 1:
                        for i in range(2):
                            c = (2 * h + i) * P
                            last = mm(ps[:, 3 + c // 512, c % 512:c % 512 + P], src_k[:, h, i * P:(i + 1) * P],
                                      src_q[:, h, i * P:(i + 1) * P], start=True, stop=True)
                        if half <= 2:
                            last = mm(ps[0:NS, 5, h * NS:(h + 1) * NS], src_k[:, h, NP:NT], src_q[:, h, NP:NT],
                                      start=True, stop=True)
                    else:
                        last = mm(ps[:, 3, h * P:(h + 1) * P], src_k[:, h, 0:P], src_q[:, h, P:NP],
                                  start=True, stop=True)
                last.then_inc(S["lvl_mm"], 1)

            def transpose_v(src, base):
                for i, (t0, r) in enumerate(TILES):
                    if base + i >= 2:
                        pe.wait_ge(S["v_ok"], base + i - 1)
                    for h in range(H):
                        last = nc.tensor.transpose(ps[0:r, 6 + (base + i) % 2, h * P:(h + 1) * P],
                                                   src[:, h, t0:t0 + r], ident)
                    last.then_inc(S["vt_mm"], 1)

            def gate_columns():
                pe.wait_ge(S["rows_ok"], 1)
                pe.wait_ge(S["lvl_ok"], 3)
                for i, (t0, r) in enumerate(TILES):
                    for q, row in enumerate((0, 2)):
                        nc.tensor.transpose(ps[0:r, 5, (2 * i + q) * H:(2 * i + q + 1) * H],
                                            rows[:, row, t0:t0 + r], ident[0:H, 0:H])
                for h in range(H):
                    g, hh = h // 2, h % 2
                    last = mm(ps[64 * hh:64 * hh + 64, 5, 64 + g * (NS + NSEQ):64 + (g + 1) * (NS + NSEQ)],
                              head_row(h, 64), r_int[:, :], start=True, stop=True)
                last.then_inc(S["rcol_mm"], 1)

            def spread_rows(h):
                pe.wait_ge(S["v_ok"], 6)
                if h:
                    pe.wait_ge(S["d_ok"], h)
                    pe.wait_ge(S["em_ok"], h)
                mm(ps[:, 6, 0:NT], head_row(h), rows[:, 5, :], start=True, stop=True)
                mm(ps[:, 7, 0:NT], head_row(h), rows[:, 1, :], start=True, stop=True).then_inc(S["rbc_mm"], 1)

            tiles = [(g, j) for g in range(3) for j in range(4)] + [(None, 0)] + \
                    [(g, j) for g in range(3, 7) for j in range(4)]
            assert len(tiles) == NPROJ
            for c, (g, j) in enumerate(tiles):
                project(c, g, j)
                if c == 13:
                    pe.wait_ge(S["proj_ok"], 12)
                    transpose_v(T[3], 0)
                if c == 19:
                    gate_columns()
                if c == 21:
                    pe.wait_ge(S["proj_ok"], 21)
                    transpose_v(va_T, 3)
                if 22 <= c < 26:
                    spread_rows(c - 22)
                if c in LVL_TILE:
                    level(LVL_TILE[c])
            pe.wait_ge(S["proj_ok"], NPROJ)
            pe.wait_ge(S["lvl_ok"], NLV)
            for h in range(H):
                g, lo = h // 2, 64 * (h % 2)
                q, k = QK[lo:lo + 64, g, :], QK[lo:lo + 64, 2 + g, :]
                mm(ps[:, h, 0:NP], k[:, 0:P], q[:, 0:NP], start=True, stop=True)
                mm(ps[:, h, NP:NP + P], k[:, P:NP], q[:, P:NP], start=True, stop=True)
                last = mm(ps[0:NS, h, 384:384 + NS], k[:, NP:NT], q[:, NP:NT], start=True, stop=True)
            last.then_inc(S["qk_mm"], 1)

            pe.wait_ge(S["d_ok"], H)
            pe.wait_ge(S["em_ok"], H)
            pe.wait_ge(S["sA_ok"], 1)
            pe.wait_ge(S["inter_ok"], 1)
            for h in range(H):
                g, lo = h // 2, 64 * (h % 2)
                out = ps[:, 4 + h, :]
                mm(out[:, 0:NP], ones, AA[:, h, 0:2, :].rearrange("p i t -> p (i t)"), start=True, stop=False)
                mm(out[:, P:NP], ones, AA[:, h, 2, :], start=False, stop=False)
                mm(out[:, NP:NT], ones[0:NS, :], AAs[:, h, :], start=False, stop=False)
                last = mm(out[:, NP:NT], ones[lo:lo + 64, :], qn[lo:lo + 64, g, :], start=False, stop=True)
            last.then_inc(S["denA_mm"], 1)

            pe.wait_ge(S["state_in"], 16 * 9)
            for h in range(H):
                g, hh = h // 2, h % 2
                v = slice(h * DV, (h + 1) * DV)
                mm(ps[:, h, 0:NP], V[:, 0, v], AA[:, h, 0:2, :].rearrange("p i t -> p (i t)"), start=True, stop=False)
                mm(ps[:, h, P:NP], V[:, 1, v], AA[:, h, 2, :], start=False, stop=hh == 1)
                mm(num_s(g)[:, :, hh, :], V[0:NS, 2, v], AAs[:, h, :].rearrange("p (b t) -> p b t", b=NSEQ),
                   start=False, stop=False)
                if hh == 1:
                    for b in range(NSEQ):
                        last = mm(ps[:, 2 * g, NP + 2 * b * TS:NP + 2 * (b + 1) * TS], C0[:, b, g, :],
                                  qi2[:, g, b, :, :].rearrange("p q t -> p (q t)"), start=False, stop=b == NSEQ - 1)
            last.then_inc(S["numA_mm"], 1)

            pe.wait_ge(S["qg_ok"], 1)
            pe.wait_ge(S["D_ok"], 1)
            for h in range(H):
                out = ps[:, 4 + h, :]
                v = slice(512 + h * DV, 512 + (h + 1) * DV)
                mm(out[:, 0:NP], V[:, 0, v], AB[:, h, 0:2, :].rearrange("p i t -> p (i t)"), start=True, stop=False)
                mm(out[:, P:NP], V[:, 1, v], AB[:, h, 2, :], start=False, stop=False)
                mm(out[:, NP:NT], V[0:NS, 2, v], ABs[:, h, :], start=False, stop=False)
                for b in range(NSEQ):
                    last = mm(out[:, NP + b * TS:NP + (b + 1) * TS], S0[:, b, h, :], qg[:, h, b * TS:(b + 1) * TS],
                              start=False, stop=b == NSEQ - 1)
            last.then_inc(S["oB_mm"], 1)

            def square_sums(sq, bank0, done):
                for n in range(3):
                    w = min(512, H * NT - n * 512)
                    last = mm(ps[:, bank0 + n, 0:w], ones, flat(sq)[:, n * 512:n * 512 + w], start=True, stop=True)
                last.then_inc(done, 1)

            pe.wait_ge(S["hA_sq"], 1)
            square_sums(T[2], 0, S["ssA_mm"])
            pe.wait_ge(S["oB_sq"], 1)
            square_sums(T[1], 5, S["ssB_mm"])

            def transpose_keys_a():
                pe.wait_ge(S["rB_ok"], 1)
                for i, (t0, r) in enumerate(TILES):
                    for g in range(2):
                        last = nc.tensor.transpose(ps[0:r, 5 + i // 2, (2 * (i % 2) + g) * P:(2 * (i % 2) + g + 1) * P],
                                                   QK[:, 2 + g, t0:t0 + r], ident)
                last.then_inc(S["kat_mm"], 1)

            def transpose_keys_b():
                pe.wait_ge(S["kd_ok"], 1)
                pe.wait_ge(S["kat_ok"], 3)
                for i, (t0, r) in enumerate(TILES):
                    for h in range(H):
                        last = nc.tensor.transpose(ps[0:r, 5 + i, h * P:(h + 1) * P], T[0][:, h, t0:t0 + r], ident)
                last.then_inc(S["kbt_mm"], 1)

            for k in range(KT):
                if k == 0:
                    pe.wait_ge(S["mixed"], 1)
                if k == KT // 2:
                    transpose_keys_a()
                    pe.wait_ge(S["mixed"], 2)
                if k == KT - 2:
                    transpose_keys_b()
                slot_ready(OUT_SLOT0 + k)
                w = ring[:, (OUT_SLOT0 + k) % RING, :]
                for i, (t0, r) in enumerate(TILES):
                    for half in range(2):
                        last = mm(out_banks(i, half), HT[:, k, t0:t0 + r], w[:, half * 512:(half + 1) * 512],
                                  start=k == 0, stop=k == KT - 1)
                last.then_inc(S["slots_used"], 1)
            pe.wait_ge(S["kbt_ok"], 3)

            pe.wait_ge(S["old_ok"], 3)

            def state_done(last):
                last.then_inc(S["st_mm"], 1)

            def prompt_states():
                for h in range(H):
                    for i in range(2):
                        last = mm(ps[:, 5, h * DV:(h + 1) * DV], KBt[:, i, h * P:(h + 1) * P],
                                  V[:, i, 512 + h * DV:512 + (h + 1) * DV], start=i == 0, stop=i == 1)
                state_done(last)
                for h in range(H):
                    g, lo = h // 2, 64 * (h % 2)
                    for i in range(2):
                        mm(ps[lo:lo + 64, 6, g * DV:(g + 1) * DV], KAt[:, i, h * DKA:(h + 1) * DKA],
                           V[:, i, h * DV:(h + 1) * DV], start=i == 0, stop=i == 1)
                    for i in range(2):
                        mm(ps[lo:lo + 64, 6, 256 + g:257 + g], KAt[:, i, h * DKA:(h + 1) * DKA],
                           ones[:, 0:1], start=i == 0, stop=i == 1)
                mm(ps[:, 6, 320:320 + 2 * NSEQ], ident, n0[:, :, :].rearrange("p g b -> p (g b)"),
                   start=True, stop=False)
                for h in range(H):
                    g, lo = h // 2, 64 * (h % 2)
                    last = mm(ps[lo:lo + 64, 6, 320 + g * NSEQ:320 + (g + 1) * NSEQ],
                              KAt[0:NS, 2, h * DKA:(h + 1) * DKA], seq_of, start=False, stop=h >= 2)
                state_done(last)

            def sample_state(n):
                b0 = 0 if n == 1 else 5
                b1 = b0 + 1
                if n >= 2:
                    pe.wait_ge(S["st_ok"], 2 + n - 1)
                heads = [n] if n < H else [2 * (n - H), 2 * (n - H) + 1]
                for q, bank in enumerate((b0, b1)):
                    old = S0[:, 4 * q:4 * q + 4, n, :] if n < H else C0[:, 4 * q:4 * q + 4, n - H, :]
                    last = mm(ps[:, bank, :], ident, old, start=True, stop=False)
                    for h in heads:
                        vb = h if n < H else H + h
                        pe.wait_ge(S["vb_ok"], vb + 1)
                        if n < H:
                            last = mm(ps[:, bank, :], KBt[0:NS, 2, h * P:(h + 1) * P],
                                      VB[vb % len(VB)][0:NS, q * 512:(q + 1) * 512], start=False, stop=True)
                        else:
                            lo = 64 * (h % 2)
                            last = mm(ps[lo:lo + 64, bank, :], KAt[0:NS, 2, h * DKA:(h + 1) * DKA],
                                      VB[vb % len(VB)][0:NS, q * 512:(q + 1) * 512], start=False, stop=True)
                last.then_inc(S["vb_used"], len(heads))
                pe.wait_ge(S["vb_used"], (heads[-1] if n < H else H + heads[-1]) + 1)
                pe.sem_inc(S["st_mm"], 1)

            def route(i):
                t0, r = TILES[i]
                pe.wait_ge(S["xT_ok"], 8 + 2 * i)
                if i == 0:
                    pe.wait_ge(S["router_in"], 32)
                if i == 2:
                    pe.wait_ge(S["logits_ok"], 1)
                for k in range(KT):
                    last = mm(ps[0:r, (4, 7, 4)[i], 0:NE], xT[:, k, t0:t0 + r], w_r[:, k, :],
                              start=k == 0, stop=k == KT - 1)
                last.then_inc(S["router_mm"], 1)

            def transpose_normed(i):
                pe.wait_ge(S["x_norm"], 4 + i)
                pe.wait_ge(S["r1_ok"], 6)
                transpose_x(i, 6, 2)

            prompt_states()
            pe.wait_ge(S["st_ok"], 2)
            sample_state(0)
            transpose_normed(0)
            route(0)
            sample_state(1)
            transpose_normed(1)
            transpose_normed(2)
            route(1)
            route(2)

            pe.wait_ge(S["pick_ok"], 3)
            for i, (_, r) in enumerate(TILES):
                for j in range(i + 1):
                    rj = TILES[j][1]
                    mm(ps[:, 4, P + i * NE:P + (i + 1) * NE], (tri if j == i else ones)[0:rj, :], pick[0:rj, j, :],
                       start=j == 0, stop=j == i)
            for j, (_, r) in enumerate(TILES):
                last = mm(ps[:, 4, P + 3 * NE:P + 4 * NE], ones[0:r, :], pick[0:r, j, :], start=j == 0, stop=j == 2)
            last.then_inc(S["rank_mm"], 1)

            def gather(b, n):
                pe.wait_ge(S["OH_ok"], n)
                for k in range(KT):
                    for q in range(9):
                        r = TILES[q % 3][1]
                        last = mm(ps[:, 7, k * BLK:(k + 1) * BLK], xb[q][0:r, k * P:(k + 1) * P], OH[0:r, q % 3, :],
                                  start=q == 0, stop=q == 8)
                last.then_inc(S["rows_mm"], 1)

            def gates_to_rows(b):
                pe.wait_ge(S["GW_ok"], b + 1)
                pe.sem_inc(S["GW_seen"], 1)
                for i, (t0, r) in enumerate(TILES):
                    last = nc.tensor.transpose(ps[0:BLK, 4, t0:t0 + r], GW[0:r, i, :], ident[0:r, 0:r])
                last.then_inc(S["gt_mm"], 1)

            def combine(b, first=False):
                pe.wait_ge(S["y_copied"], b + 1)
                pe.wait_ge(S["GT_ok"], b * 2 + 2)
                for n, (bank, need) in enumerate(zip(CB_BANKS, CB_NEEDS)):
                    if need or not first:
                        pe.wait_ge(S["cb_added"], b * 5 + need)
                        pe.sem_inc(S["cb_seen"], 1)
                    i, half = (n // 2, n % 2) if n < 4 else (2, 0)
                    for half in (0, 1) if n == 4 else (half,):
                        t0, r = TILES[i]
                        lo = 64 * half if n == 4 else 0
                        last = mm(ps[lo:lo + r, bank, :], GT[64 * half:64 * half + BLK, t0:t0 + r],
                                  y_s[64 * half:64 * half + BLK, :], start=True, stop=True)
                    last.then_inc(S["cb_mm"], 1)

            def ple_products(c, phase):
                if phase == 0:
                    pe.wait_ge(S["ple_w_in"], c * 32 + 32)
                for k in range(4 * phase, 4 * phase + 4):
                    mm(ps[:, 5, 0:NT], ple_w[:, k, :], xT[:, k, :], start=k == 0, stop=k == KT - 1)
                if phase == 1:
                    pe.wait_ge(S["cb_added"], c * 10 + 5 * (HEAD_BLOCKS + 1))
                    for k in range(2):
                        last = mm(ps[:, 6, 0:NT], ple_w[:, KT + k, :], pT[:, k, :], start=k == 0, stop=k == 1)
                    last.then_inc(S["ple_used"], 1)

            def ple_transposes(c):
                pe.wait_ge(S["ple_prod"], c + 1)
                pe.sem_inc(S["ple_seen"], 1)
                for i, (t0, r) in enumerate(TILES):
                    last = nc.tensor.transpose(ps[0:r, 2, i * P:(i + 1) * P], ple[:, t0:t0 + r], ident)
                last.then_inc(S["ple_t"], 1)

            def expert_block(b, ahead, before=None, between=None, after=None, combines=True):
                if not ahead and before:
                    before()
                pe.wait_ge(S["xTe_ok"], b + 1)
                pe.wait_ge(S["sel_ok"], b + 1)
                pe.wait_ge(S["gu_free"], b + 1)
                for w in range(2):
                    for half in range(2):
                        mm(ps[64 * half:64 * half + 64, w, :], sel[:, :], bias3[:, w, half * 512:(half + 1) * 512],
                           start=True, stop=False)
                for k in range(KT):
                    for w in range(2):
                        j = 2 * k + w
                        s = (PRE + j) % RING
                        pe.wait_ge(slot_full[s], b * (16 * PER // RING) + 16 * ((PRE + j) // RING + 1))
                        for half in range(2):
                            last = mm(ps[64 * half:64 * half + 64, w, :], xTe[:, k, :],
                                      ring[:, s, half * 512:(half + 1) * 512], start=False, stop=k == KT - 1)
                        last.then_inc(S["slots_used"], 1)
                if ahead:
                    gather(b + 1, b + 2)
                if ahead and before:
                    before()
                gates_to_rows(b)
                if between:
                    between()
                if combines:
                    pe.wait_ge(S["cb_added"], b * 5 - 2)
                pe.wait_ge(S["h_ok"], b + 1)
                for j in range(4):
                    last = nc.tensor.transpose(ps[:, 3, j * P:(j + 1) * P], h_s[:, j * P:(j + 1) * P], ident)
                last.then_inc(S["ht_mm"], 1)
                pe.wait_ge(S["GT_ok"], b * 2 + 2)
                for half in range(2):
                    mm(ps[64 * half:64 * half + 64, 4, :], sel[:, :], bias3[:, 2, half * 512:(half + 1) * 512],
                       start=True, stop=False)
                pe.wait_ge(S["hTe_ok"], b + 1)
                for k in range(KT):
                    j = 2 * KT + k
                    s = (PRE + j) % RING
                    pe.wait_ge(slot_full[s], b * (16 * PER // RING) + 16 * ((PRE + j) // RING + 1))
                    for half in range(2):
                        last = mm(ps[64 * half:64 * half + 64, 4, :],
                                  hTe[:, k % 4, (k // 4) * BLK:(k // 4 + 1) * BLK],
                                  ring[:, s, half * 512:(half + 1) * 512], start=False, stop=k == KT - 1)
                    last.then_inc(S["slots_used"], 1)
                if after:
                    after()

            gather(0, 1)
            for b in range(HEAD_BLOCKS):
                def before():
                    if b:
                        combine(b - 1, b == 1)
                        pe.wait_ge(S["cb_added"], 5 * b)
                    sample_state(2 + b)
                expert_block(b, True, before, combines=b > 0)

            pe.wait_ge(S["st_ok"], 8)
            pe.wait_ge(S["p_in"], 48)
            for i, (t0, r) in enumerate(TILES):
                for g in range(2):
                    last = nc.tensor.transpose(ps[:, 5 + g, t0:t0 + r], p_in[0:r, i, g * P:(g + 1) * P], ident[0:r, 0:r])
            last.then_inc(S["pt_mm"], 1)
            pe.sem_inc(S["ple_used"], 1)
            pe.wait_ge(S["pT_ok"], 1)
            with pe.Fori(0, KT) as c:
                b = c * 2 + HEAD_BLOCKS

                def combine_ple():
                    pe.wait_ge(S["ple_added"], c + 1)
                    combine(c * 2 + (HEAD_BLOCKS - 1))
                expert_block(b, True, combine_ple, lambda: ple_products(c, 0))
                b1 = c * 2 + (HEAD_BLOCKS + 1)
                expert_block(b1, True, lambda: combine(c * 2 + HEAD_BLOCKS), lambda: ple_products(c, 1),
                             lambda: ple_transposes(c))
            pe.wait_ge(S["ple_added"], KT + 1)
            with pe.Fori(PLE_END, NE - 1) as b:
                expert_block(b, True, lambda: combine(b - 1))
            expert_block(NE - 1, False, lambda: combine(NE - 2))
            combine(NE - 1)
            pe.wait_ge(S["cb_added"], 5 * NE)
            extra = pe.value_load(n_exti[0:1, 0:1], min_val=0, max_val=NEXTRA)
            with pe.If(extra > 0):
                with pe.Fori(0, NEXTRA) as j:
                    with pe.If(extra > j):
                        gather(j + NE, j + (NE + 2))
                        expert_block(j + NE, False, combines=False)
                        combine(j + NE)

        @block.scalar
        def _(act):
            step = Steps(act, S["act_steps"])

            def f(out, in_, func, **kw):
                return nc.scalar.activation(out, in_, func, **kw)

            def norm_scale(i, n):
                act.wait_ge(S["ln_var"], n)
                r = TILES[i][1]
                step(f(mv[0:r, i, 2:3], mv[0:r, i, 1:2], ACT.Ln, bias=eps[0:r, 0:1]))
                f(mv[0:r, i, 3:4], mv[0:r, i, 2:3], ACT.Exp, scale=-0.5).then_inc(S["ln_rstd"], 1)

            def copy_xT(i, first, bank0):
                t0, r = TILES[i]
                for q in range(2):
                    act.wait_ge(S["xt_mm"], first + 2 * i + q + 1)
                    f(xT[:, 4 * q:4 * q + 4, t0:t0 + r], ps[:, bank0 + q, 0:4 * r].rearrange("p (k t) -> p k t", k=4),
                      ACT.Copy).then_inc(S["xT_ok"], 1)

            act.wait_ge(S["setup"], 1)
            for i in range(3):
                norm_scale(i, i + 1)
                if i:
                    copy_xT(i - 1, 0, 6)
            copy_xT(2, 0, 6)

            def copy_values(base, off):
                for i, (_, r) in enumerate(TILES):
                    act.wait_ge(S["vt_mm"], base + i + 1)
                    f(V[0:r, i, off:off + 512], ps[0:r, 6 + (base + i) % 2, :], ACT.Copy).then_inc(S["v_ok"], 1)

            dest = [(G, j) for j in range(4)] + [(QB, j) for j in range(4)] + [(T[3], j) for j in range(4)] + \
                   [(None, 0)] + [(QK, j) for j in range(4)] + [(va_T, j) for j in range(4)] + \
                   [(GB, j) for j in range(4)] + [(OA, j) for j in range(4)]

            def decays(n):
                w = T[n % 2][:, :, :] if n < NLV - 1 else T[n % 2][:, :, 0:NP]
                act.wait_ge(S["sub_ok"], n)
                step(f(w, w, ACT.Abs))
                f(w, w, ACT.Exp, scale=-1.0).then_inc(S["w_ok"], 1)

            for c, (buf, j) in enumerate(dest):
                act.wait_ge(S["proj_mm"], c + 1)
                if c == 8:
                    act.wait_ge(S["bias_ok"], 1)
                if c == 25:
                    act.wait_ge(S["g_ok"], 1)
                    act.wait_ge(S["rows_ok"], 1)
                if buf is None:
                    step(f(rows[:, 0, :], ps[0:H, c % 3, 0:NT], ACT.Copy))
                    f(rows[:, 1, :], ps[32:32 + H, c % 3, 0:NT], ACT.Copy).then_inc(S["proj_ok"], 1)
                else:
                    f(buf[:, j, :], ps[:, c % 3, 0:NT], ACT.Copy,
                      scale=DKA ** -0.5 if buf is QK and j >= 2 else 1.0).then_inc(S["proj_ok"], 1)
                if c == 4:
                    act.wait_ge(S["z_ok"], 1)
                    f(T[0][:, :, :], G[:, :, :], ACT.Exp, scale=-1.0).then_inc(S["e_ok"], 1)
                    act.wait_ge(S["lb_max"], 1)
                    f(lb[:, 1, :], lb[:, 1, :], ACT.Exp).then_inc(S["lb_exp"], 1)
                if c == 7:
                    act.wait_ge(S["proj_ok"], 8)
                    f(T[2][:, :, :], QB[:, :, :], ACT.Exp, scale=-1.0).then_inc(S["eq_ok"], 1)
                if c == 8:
                    act.wait_ge(S["f_ok"], 1)
                    f(G[:, :, :], G[:, :, :], ACT.Ln).then_inc(S["lnf_ok"], 1)
                if c == 12:
                    decays(1)
                if c == 13:
                    copy_values(0, 512)
                    act.wait_ge(S["f_rows"], 1)
                    step(f(rows[:, 2, :], rows[:, 1, :], ACT.Abs))
                    step(f(rows[:, 2, :], rows[:, 2, :], ACT.Exp, scale=-1.0))
                    f(rows[:, 2, :], rows[:, 2, :], ACT.Ln, bias=eps[0:H, 2:3]).then_inc(S["sp_rows"], 1)
                if c == 14:
                    decays(2)
                if c == 16:
                    decays(3)
                    act.wait_ge(S["m_rows"], 1)
                    step(f(rows[:, 2, :], rows[:, 2, :], ACT.Exp))
                    step(f(r_int[:, :], r_int[:, :], ACT.Exp))
                    f(rows[:, 1, :], rows[:, 3, :], ACT.Exp, scale=-1.0).then_inc(S["rows_ok"], 1)
                if c == 18:
                    decays(4)
                if c == 20:
                    decays(5)
                if c == 21:
                    copy_values(3, 0)
                if 22 <= c < 26:
                    act.wait_ge(S["rbc_mm"], c - 21)
                    f(EM[:, c - 22, :], ps[:, 7, 0:NT], ACT.Copy).then_inc(S["em_ok"], 1)
                if c == 22:
                    decays(6)
                if c == 24:
                    decays(7)
                if c == 26:
                    decays(8)
                    act.wait_ge(S["d_ok"], H)
                    step(f(AA[:, :, :, :], AA[:, :, :, :], ACT.Exp))
                    f(AAs[:, :, :], AAs[:, :, :], ACT.Exp).then_inc(S["d_exp"], 1)
                    step(f(qg[:, :, :], G[:, :, NP:NT], ACT.Exp))
                    f(decB[:, :, :], G[:, :, NP + TS - 1:NT:TS], ACT.Exp).then_inc(S["gexp"], 1)

            act.wait_ge(S["proj_ok"], NPROJ)
            act.wait_ge(S["lvl_ok"], NLV)
            f(T[2][:, :, :], GB[:, :, :], ACT.Sigmoid).then_inc(S["gates_sig"], 1)
            f(T[3][:, :, :], OA[:, :, :], ACT.Sigmoid).then_inc(S["gates_sig"], 1)
            act.wait_ge(S["hA_ok"], 1)
            f(T[2][:, :, :], EM[:, :, :], ACT.Square).then_inc(S["hA_sq"], 1)
            act.wait_ge(S["oB_mm"], 1)
            step(f(T[0][:, :, :], ps[:, 4:8, 0:NT], ACT.Copy))
            f(T[1][:, :, :], T[0][:, :, :], ACT.Square).then_inc(S["oB_sq"], 1)

            def inverse_rms(dst, bank0, done):
                sums = ps[:, bank0:bank0 + 3, :].rearrange("p b n -> p (b n)")[:, 0:H * NT]
                step(f(flat(dst), sums, ACT.Ln, scale=1.0 / DV, bias=eps[:, 1:2]))
                f(flat(dst), flat(dst), ACT.Exp, scale=-0.5).then_inc(done, 1)

            act.wait_ge(S["ssA_mm"], 1)
            inverse_rms(QB, 0, S["rA_ok"])
            act.wait_ge(S["ssB_mm"], 1)
            inverse_rms(T[1], 5, S["rB_ok"])
            act.wait_ge(S["mixed"], 2)
            for h in range(H):
                f(T[0][:, h, 0:NP], G[:, h, 0:NP], ACT.Exp, scale=-1.0, bias=G[:, h, NP - 1:NP]).then_inc(S["kd_exp"], 1)
            act.wait_ge(S["kd_sub"], 1)
            f(T[0][:, :, NP:NT], T[0][:, :, NP:NT], ACT.Exp).then_inc(S["kd_exp"], 1)
            act.wait_ge(S["kbt_mm"], 1)
            for i, (_, r) in enumerate(TILES):
                f(KBt[0:r, i, :], ps[0:r, 5 + i, :], ACT.Copy).then_inc(S["kbt_ok"], 1)

            def state_out(n):
                act.wait_ge(S["st_mm"], n + 1)
                if n == 0:
                    f(sp_s, ps[:, 5, :], ACT.Copy).then_inc(S["st_ok"], 1)
                elif n == 1:
                    step(f(cp_s, ps[:, 6, 0:256], ACT.Copy))
                    step(f(np_s[:, 0:2], ps[:, 6, 256:258], ACT.Copy))
                    f(np_s[:, 2:2 + 2 * NSEQ], ps[:, 6, 320:320 + 2 * NSEQ], ACT.Copy).then_inc(S["st_ok"], 1)
                else:
                    m = n - 2
                    b0 = 0 if m == 1 else 5
                    dst = S0[:, :, m, :] if m < H else C0[:, :, m - H, :]
                    f(dst, ps[:, b0:b0 + 2, :].rearrange("p q (b v) -> p (q b) v", b=4), ACT.Copy).then_inc(S["st_ok"], 1)

            def gates(i):
                r = TILES[i][1]
                act.wait_ge(S["top_ok"], i + 1)
                f(gate[0:r, i, :], top_v[0:r, i, 0:TOPK], ACT.Exp, bias=neg_v[0:r, i:i + 1],
                  accum_out=gsum[0:r, i:i + 1]).then_inc(S["gate_exp"], 1)

            state_out(0)
            state_out(1)
            norm_scale(0, 4)
            state_out(2)
            norm_scale(1, 5)
            copy_xT(0, 6, 2)
            norm_scale(2, 6)
            state_out(3)
            copy_xT(1, 6, 2)
            copy_xT(2, 6, 2)
            for i in range(3):
                gates(i)
            def store_states():
                act.wait_ge(S["st_ok"], 8)
                with nc.allow_non_contiguous_dma(reason="small states laid out by partition"):
                    for h in range(H):
                        g, lo = h // 2, 64 * (h % 2)
                        act.dma_start(o[6][0, :, h].rearrange("b d v -> d b v"), C0[lo:lo + 64, :, g, :]).then_inc(S["st_out"], 16)
                    act.dma_start(o[4][0].rearrange("b h -> h b"), rows[:, 3, NP - 1:NP]).then_inc(S["st_out"], 16)
                    act.dma_start(o[8][0].rearrange("b h -> h b"), rows[:, 3, NP + TS - 1:NT:TS]).then_inc(S["st_out"], 16)
                    act.dma_start(o[9][0].rearrange("b h d v -> d (b h) v"),
                                  S0[:, :, :, :].rearrange("p b h v -> p (b h) v")).then_inc(S["st_out"], 16)

            def copy_rows(b):
                act.wait_ge(S["rows_mm"], b + 1)
                f(xTe[:, :, :], ps[:, 7, :].rearrange("p (k s) -> p k s", k=KT), ACT.Copy).then_inc(S["xTe_ok"], 1)

            def expert_block(b, ahead, before=None, after=None):
                act.wait_ge(S["g_ready"], b + 1)
                f(sg_s, g_s, ACT.Sigmoid, scale=SWIGLU_ALPHA).then_inc(S["sg_ok"], 1)
                if ahead:
                    copy_rows(b + 1)
                if before:
                    before()
                act.wait_ge(S["gt_mm"], b + 1)
                for lo in (0, BLK):
                    f(GT[lo:lo + BLK, :], ps[0:BLK, 4, 0:NT], ACT.Copy).then_inc(S["GT_ok"], 1)
                act.wait_ge(S["ht_mm"], b + 1)
                f(hTe[:, :, :], ps[:, 3, :].rearrange("p (j s) -> p j s", j=4), ACT.Copy).then_inc(S["hTe_ok"], 1)
                if after:
                    after()
                act.wait_ge(S["slots_used"], b * PER + (PRE + PER))
                f(y_s, ps[:, 4, :], ACT.Copy).then_inc(S["y_copied"], 1)

            copy_rows(0)
            act.wait_ge(S["st_ok"], 2)
            with nc.allow_non_contiguous_dma(reason="small states laid out by partition"):
                act.dma_start(o[5][0, 0].rearrange("h d v -> d h v"), sp_s.rearrange("p (h v) -> p h v", h=H)).then_inc(S["t3_out"], 16)
                for h in range(H):
                    g, lo = h // 2, 64 * (h % 2)
                    act.dma_start(o[2][0, 0, h], cp_s[lo:lo + 64, g * DV:(g + 1) * DV]).then_inc(S["t3_out"], 16)
                    act.dma_start(o[3][0, 0, h:h + 1].rearrange("o d -> d o"), np_s[lo:lo + 64, g:g + 1]).then_inc(S["t3_out"], 16)
                    act.dma_start(o[7][0, :, h].rearrange("b d -> d b"),
                                  np_s[lo:lo + 64, 2 + g * NSEQ:2 + (g + 1) * NSEQ]).then_inc(S["t3_out"], 16)
            act.wait_ge(S["t3_out"], 16 * 13)
            for b in range(HEAD_BLOCKS):
                expert_block(b, True, lambda: state_out(4 + b))
            act.wait_ge(S["pt_mm"], 1)
            f(pT[:, :, :], ps[:, 5:7, 0:NT], ACT.Copy).then_inc(S["pT_ok"], 1)
            store_states()

            def ple_gate(c):
                act.wait_ge(S["ple_used"], c + 2)
                f(ple, ps[:, 5, 0:NT], ACT.Sigmoid).then_inc(S["ple_sig"], 1)

            with act.Fori(0, KT) as c:
                expert_block(c * 2 + HEAD_BLOCKS, True)
                expert_block(c * 2 + (HEAD_BLOCKS + 1), True, after=lambda: ple_gate(c))
            with act.Fori(PLE_END, NE - 1) as b:
                expert_block(b, True)
            expert_block(NE - 1, False)
            extra = act.value_load(n_exti[0:1, 0:1], min_val=0, max_val=NEXTRA)
            with act.If(extra > 0):
                with act.Fori(0, NEXTRA) as j:
                    with act.If(extra > j):
                        copy_rows(j + NE)
                        expert_block(j + NE, False)
            act.wait_ge(S["st_out"], 16 * 7)
            for i in range(3):
                norm_scale(i, 7 + i)

        @block.vector
        def _(dve):
            step = Steps(dve, S["dve_steps"])
            tt, ts, stt = nc.vector.tensor_tensor, nc.vector.tensor_scalar, nc.vector.scalar_tensor_tensor

            step(nc.vector.memset(eps[:, 0:1], LN_EPS))
            step(nc.vector.memset(eps[:, 1:2], NORM_EPS))
            nc.vector.memset(eps[:, 2:3], 1.0).then_inc(S["setup"], 1)

            def norm_stats(i, n):
                r = TILES[i][1]
                x = xs[0:r, i, :]
                for q in range(2):
                    step(nc.vector.bn_stats(lns[0:r, i, q, :], x[:, q * 512:(q + 1) * 512]))
                if n > 3:
                    dve.wait_ge(S["ln_rstd"], n - 3)
                nc.vector.bn_aggr(mv[0:r, i, 0:2], lns[0:r, i, :, :].rearrange("p q s -> p (q s)")).then_inc(S["ln_var"], 1)

            def norm_apply(i, n):
                r = TILES[i][1]
                x = xs[0:r, i, :]
                dve.wait_ge(S["ln_var"], n)
                step(stt(x, x, mv[0:r, i, 0:1], ln_g[0:r, :], ALU.subtract, ALU.mult))
                dve.wait_ge(S["ln_rstd"], n)
                stt(x, x, mv[0:r, i, 3:4], ln_b[0:r, :], ALU.mult, ALU.add).then_inc(S["x_norm"], 1)
                dve.wait_ge(S["x_norm"], n)

            def norm(i, n):
                norm_stats(i, n)
                norm_apply(i, n)

            for i in range(3):
                dve.wait_ge(S[f"x_in{i}"], 16)
                if i == 0:
                    dve.wait_ge(S["ln1_in"], 32)
                norm(i, i + 1)

            step(nc.vector.memset(flat(reset), 1.0))
            step(nc.vector.memset(reset[:, :, 0:1], 0.0))
            step(nc.vector.memset(reset[:, :, NP:NT:TS], 0.0))
            step(nc.vector.memset(oneh[:, :, :, :], 0.0))
            step(nc.vector.memset(AB[:, :, :, :], 0.0))
            step(nc.vector.memset(ABs[:, :, :], 0.0))
            step(nc.vector.memset(m0[:, 0:1], 0.0))
            step(nc.vector.memset(pick[:, :, :], 0.0))
            step(nc.vector.memset(qi2[:, :, :, :, :], 0.0))
            dve.wait_ge(S["const_in"], 16)
            step(nc.vector.tensor_copy(blk_e[:, 0:NE], iota))
            step(nc.vector.memset(gate[:, :, :], 0.0))
            step(nc.vector.memset(row_of[:, :, :], -1.0))
            step(nc.vector.memset(gate_of[:, :, :], 0.0))
            dve.wait_ge(S["mask_in"], 16)
            step(nc.vector.tensor_copy(masks[:, :], flat(T[3])))
            dve.wait_ge(S["bias_in"], 48)
            for n in range(3):
                b, part = view(T[n], 0, D)[0:NE, :], view(T[3], 0, D)[0:NE, :]
                step(nc.vector.tensor_copy(bias3[0:NE, n, :], b))
                step(tt(part, b, bias3[0:NE, n, :], ALU.subtract))
                step(nc.vector.tensor_copy(sel2[0:NE, :], part))
                step(nc.vector.tensor_copy(bias3[NE:2 * NE, n, :], sel2[0:NE, :]))
                step(tt(part, part, sel2[0:NE, :], ALU.subtract))
                step(nc.vector.tensor_copy(bias3[2 * NE:3 * NE, n, :], part))
            dve.sem_inc(S["bias_ok"], 1)

            dve.wait_ge(S["vec_in"], 16 * 6)
            tt(lb[:, 1, :], lb[:, 0, :], lb[:, 0, :], ALU.subtract).then_inc(S["lb_max"], 1)
            dve.wait_ge(S["proj_ok"], 4)
            ts(G[:, :, :], G[:, :, :], -43.5, None, ALU.max).then_inc(S["z_ok"], 1)
            dve.wait_ge(S["lb_exp"], 1)
            step(nc.vector.reciprocal(lb[:, 2, :], lb[:, 1, :]))
            step(tt(lb[:, 2, :], lb[:, 1, :], lb[:, 2, :], ALU.mult))
            step(tt(lb[:, 3, :], lb[:, 2, :], lb[:, 2, :], ALU.subtract))
            step(ts(lb[:, 4, :], lb[:, 3, :], -1.0, 1.0, ALU.mult, ALU.add))
            step(ts(lb[:, 5, :], lb[:, 3, :], LB_FLOOR, None, ALU.max))
            dve.wait_ge(S["e_ok"], 1)
            step(ts(T[1][:, :, :], T[0][:, :, :], 1.0, None, ALU.add))
            step(nc.vector.reciprocal(T[1][:, :, :], T[1][:, :, :]))
            for h in range(H):
                step(ts(G[:, h, :], T[1][:, h, :], lb[:, 4, h:h + 1], lb[:, 5, h:h + 1], ALU.mult, ALU.add))
            dve.sem_inc(S["f_ok"], 1)
            for h in range(H):
                step(stt(KB[:, h, :], T[0][:, h, :], lb[:, 4, h:h + 1], T[1][:, h, :], ALU.mult, ALU.mult))
            dve.wait_ge(S["lnf_ok"], 1)
            nc.vector.tensor_tensor_scan(flat(G), flat(reset), flat(G), 0.0, ALU.mult, ALU.add).then_inc(S["g_ok"], 1)
            dve.wait_ge(S["g_ok"], 1)
            dve.wait_ge(S["eq_ok"], 1)
            step(ts(T[2][:, :, :], T[2][:, :, :], 1.0, None, ALU.add))
            step(nc.vector.reciprocal(T[2][:, :, :], T[2][:, :, :]))
            tt(QB[:, :, :], QB[:, :, :], T[2][:, :, :], ALU.mult).then_inc(S["mix_ok"], 1)
            dve.wait_ge(S["mix_ok"], 1)

            def sub(n):
                if n < NLV - 1:
                    half = 1 << (n - 1)
                    if half <= 16:
                        g = flat(G).rearrange("p (b m) -> p b m", m=2 * half)
                        w = flat(T[n % 2]).rearrange("p (b m) -> p b m", m=2 * half)
                        nb = H * NT // (2 * half)
                        tt(w, g, g[:, :, half - 1:half].to_broadcast([P, nb, 2 * half]),
                           ALU.subtract).then_inc(S["sub_ok"], 1)
                    else:
                        nb = NP // (2 * half)
                        g = G[:, :, 0:NP].rearrange("p h (b m) -> p h b m", m=2 * half)
                        w = T[n % 2][:, :, 0:NP].rearrange("p h (b m) -> p h b m", m=2 * half)
                        step(nc.vector.memset(T[n % 2][:, :, NP:NT], 0.0))
                        tt(w, g, g[:, :, :, half - 1:half].to_broadcast([P, H, nb, 2 * half]),
                           ALU.subtract).then_inc(S["sub_ok"], 1)
                else:
                    tt(T[n % 2][:, :, 0:NP], G[:, :, 0:NP], G[:, :, P - 1:P].to_broadcast([P, H, NP]),
                       ALU.subtract).then_inc(S["sub_ok"], 1)

            def mix(n):
                w, x = T[n % 2], T[2 + n % 2]
                dve.wait_ge(S["w_ok"], n)
                if n >= 3:
                    dve.wait_ge(S["lvl_mm"], n - 1)
                if n == 1:
                    dve.wait_ge(S["vt_mm"], 3)
                half = 1 << (n - 1)
                if half <= 16:
                    def parts(b):
                        return flat(b).rearrange("p (b m) -> p b m", m=2 * half)
                    lo, hi = (slice(None), slice(None), slice(0, half)), (slice(None), slice(None), slice(half, 2 * half))
                else:
                    def parts(b):
                        return b[:, :, 0:NP].rearrange("p h (b m) -> p h b m", m=2 * half)
                    lo = (slice(None),) * 3 + (slice(0, half),)
                    hi = (slice(None),) * 3 + (slice(half, 2 * half),)
                step(tt(parts(x)[lo], parts(KB)[lo], parts(w)[lo], ALU.mult))
                tt(parts(x)[hi], parts(QB)[hi], parts(w)[hi], ALU.mult).then_inc(S["mix_ok"], 1)
                dve.wait_ge(S["mix_ok"], n + 1)

            def take(n):
                dve.wait_ge(S["lvl_mm"], n + 1)
                if n < NLV - 1:
                    if n <= 2:
                        step(nc.vector.copy_predicated(ABs[:, :, :], mask(n)[0:NS, 0:NS].unsqueeze(1).to_broadcast([NS, H, NS]),
                                                       ps[0:NS, 5, 0:H * NS].rearrange("p (h t) -> p h t", h=H)))
                    for q in range(2):
                        last = nc.vector.copy_predicated(
                            AB[:, 2 * q:2 * q + 2, 0:3:2, :],
                            mask(n).unsqueeze(1).unsqueeze(1).to_broadcast([P, 2, 2, P]),
                            ps[:, 3 + q, :].rearrange("p (h i t) -> p h i t", h=2, i=2))
                        if q == 0:
                            step(last)
                else:
                    last = nc.vector.tensor_copy(AB[:, :, 1, :], ps[:, 3, :].rearrange("p (h t) -> p h t", h=H))
                last.then_inc(S["lvl_ok"], 1)
                dve.wait_ge(S["lvl_ok"], n + 1)

            def gate_rows():
                fl, ir, w, m, b, bm = (rows[:, q, :] for q in (1, 0, 2, 3, 4, 5))
                st = rows[:, :, 0:NT]
                dve.wait_ge(S["proj_ok"], 13)
                step(ts(ir, ir, r_bias[:, 0:1], None, ALU.add))
                ts(fl, fl, r_bias[:, 1:2], None, ALU.add).then_inc(S["f_rows"], 1)

            def gate_rows2():
                fl, ir, w, m, b, bm = (rows[:, q, :] for q in (1, 0, 2, 3, 4, 5))
                dve.wait_ge(S["sp_rows"], 1)
                step(stt(fl, fl, 0.0, w, ALU.min, ALU.subtract))
                step(nc.vector.tensor_tensor_scan(b, reset[0:H, 0, :], fl, 0.0, ALU.mult, ALU.add))
                step(nc.vector.tensor_copy(w, ir))
                starts = ((slice(0, 1), slice(0, 1)), (slice(NP, NT, TS), slice(1, 1 + NSEQ)))
                for src, dst in starts:
                    step(tt(r_start[:, dst], fl[:, src], m0[:, dst], ALU.add))
                    step(tt(w[:, src], w[:, src], r_start[:, dst], ALU.max))
                    step(nc.vector.memset(fl[:, src], -1.0e30))
                step(nc.vector.tensor_tensor_scan(m, fl, w, -1.0e30, ALU.add, ALU.max))
                step(tt(bm, b, m, ALU.subtract))
                step(tt(ir, ir, b, ALU.subtract))
                step(tt(w[:, 0:NP], ir[:, 0:NP], bm[:, NP - 1:NP].to_broadcast([H, NP]), ALU.add))
                ws, bs, irs = (q[:, NP:NT].rearrange("p (b t) -> p b t", b=NSEQ) for q in (w, bm, ir))
                step(tt(ws, irs, bs[:, :, TS - 1:TS].to_broadcast([H, NSEQ, TS]), ALU.add))
                mb = m0[:, 1:1 + NSEQ]
                step(tt(r_int[:, 0:NS].rearrange("p (b t) -> p b t", b=NSEQ), bs,
                        mb.unsqueeze(2).to_broadcast([H, NSEQ, TS]), ALU.add))
                tt(r_int[:, NS:NS + NSEQ], bm[:, NP + TS - 1:NT:TS], mb, ALU.add).then_inc(S["m_rows"], 1)

            def gate_cols():
                dve.wait_ge(S["rcol_mm"], 1)
                step(nc.vector.tensor_copy(cols[:, 0:2, :, :], ps[:, 5, 0:4 * H].rearrange("p (i q h) -> p i q h", i=2, q=2)))
                step(nc.vector.tensor_copy(cols[0:NS, 2, :, :], ps[0:NS, 5, 4 * H:6 * H].rearrange("p (q h) -> p q h", q=2)))
                step(nc.vector.tensor_copy(inter[:, :, :], ps[:, 5, 64:64 + 2 * (NS + NSEQ)].rearrange("p (g c) -> p g c", g=2)))
                dve.wait_ge(S["state_in"], 16 * 9)
                tt(qi[:, :, :], QK[:, 0:2, NP:NT], inter[:, :, 0:NS], ALU.mult).then_inc(S["inter_ok"], 1)
                dve.wait_ge(S["inter_ok"], 1)
                for hh in range(2):
                    rows64 = slice(64 * hh, 64 * hh + 64)
                    for g in range(2):
                        step(nc.vector.tensor_copy(qi2[rows64, g, :, hh, :],
                                                   qi[rows64, g, :].rearrange("p (b t) -> p b t", b=NSEQ)))
                step(tt(qn[:, :, :].rearrange("p g (b t) -> p g b t", b=NSEQ),
                        qi[:, :, :].rearrange("p g (b t) -> p g b t", b=NSEQ),
                        n0[:, :, :].unsqueeze(3).to_broadcast([P, 2, NSEQ, TS]), ALU.mult))

            def score_decay(h):
                dve.wait_ge(S["rbc_mm"], h + 1)
                step(ts(AA[:, h, 0:2, :].rearrange("p i t -> p (i t)"), ps[:, 6, 0:NP], cols[:, 0, 0, h:h + 1], 0.0, ALU.add, ALU.min))
                step(ts(AA[:, h, 2, :], ps[:, 6, P:NP], cols[:, 1, 0, h:h + 1], 0.0, ALU.add, ALU.min))
                ts(AAs[:, h, :], ps[0:NS, 6, NP:NT], cols[0:NS, 2, 0, h:h + 1], 0.0, ALU.add, ALU.min).then_inc(S["d_ok"], 1)
                dve.wait_ge(S["d_ok"], h + 1)

            sub(1)
            sub(2)
            take(0)
            gate_rows()
            mix(1)
            gate_rows2()
            take(1)
            for n in range(2, NLV):
                if n < NLV - 1:
                    sub(n + 1)
                mix(n)
                if n == 4:
                    gate_cols()
                if n == 5:
                    dve.wait_ge(S["vt_mm"], 6)
                    score_decay(0)
                if n == 6:
                    score_decay(1)
                if n == 7:
                    score_decay(2)
                    score_decay(3)
                if n < NLV - 1:
                    take(n)
            dve.wait_ge(S["d_exp"], 1)
            step(tt(scores(AA).rearrange("p h i t -> p h i t"), scores(AA),
                    tri.unsqueeze(1).unsqueeze(1).to_broadcast([P, H, 2, P]), ALU.mult))
            step(tt(AAs[:, :, :], AAs[:, :, :],
                    mask(1 + len(LEVELS))[0:NS, 0:NS].unsqueeze(1).to_broadcast([NS, H, NS]), ALU.mult))
            dve.wait_ge(S["gexp"], 1)
            tt(qg[:, :, :], qg[:, :, :], QB[:, :, NP:NT], ALU.mult).then_inc(S["qg_ok"], 1)
            dve.sem_inc(S["decB_ok"], 1)
            take(NLV - 1)

            dve.wait_ge(S["qk_mm"], 1)
            step(tt(AA[:, :, :, :].rearrange("p h i t -> p h (i t)"), AA[:, :, :, :].rearrange("p h i t -> p h (i t)"),
                    ps[:, 0:H, 0:384], ALU.mult))
            tt(AAs[:, :, :], AAs[:, :, :], ps[0:NS, 0:H, 384:384 + NS], ALU.mult).then_inc(S["sA_ok"], 1)
            dve.wait_ge(S["gates_sig"], 2)
            step(tt(GB[:, :, :], GB[:, :, :], T[2][:, :, :], ALU.mult))
            dve.wait_ge(S["denA_mm"], 1)
            step(stt(EM[:, :, :], ps[:, 4:8, 0:NT], -1.0, EM[:, :, :], ALU.mult, ALU.max))
            tt(EM[:, :, :], EM[:, :, :], ps[:, 4:8, 0:NT], ALU.max).then_inc(S["D_ok"], 1)
            dve.wait_ge(S["D_ok"], 1)
            step(nc.vector.reciprocal(QB[:, :, :], EM[:, :, :]))
            dve.wait_ge(S["numA_mm"], 1)
            step(tt(EM[:, :, 0:NP], QB[:, :, 0:NP], ps[:, 0:H, 0:NP], ALU.mult))
            for h in range(H):
                last = tt(EM[:, h, NP:NT].rearrange("p (b t) -> p b t", b=NSEQ),
                          QB[:, h, NP:NT].rearrange("p (b t) -> p b t", b=NSEQ), num_s(h // 2)[:, :, h % 2, :], ALU.mult)
                if h < H - 1:
                    step(last)
            last.then_inc(S["hA_ok"], 1)
            dve.wait_ge(S["hA_ok"], 1)
            dve.wait_ge(S["rA_ok"], 1)
            step(tt(EM[:, :, :], EM[:, :, :], QB[:, :, :], ALU.mult))
            for h in range(H):
                last = stt(HT[:, h, :], EM[:, h, :], gains[:, 0, h:h + 1], T[3][:, h, :], ALU.mult, ALU.mult)
                if h < H - 1:
                    step(last)
            last.then_inc(S["mixed"], 1)
            dve.wait_ge(S["rB_ok"], 1)
            step(tt(T[0][:, :, :], T[0][:, :, :], T[1][:, :, :], ALU.mult))
            for h in range(H):
                last = stt(HT[:, H + h, :], T[0][:, h, :], gains[:, 1, h:h + 1], GB[:, h, :], ALU.mult, ALU.mult)
                if h < H - 1:
                    step(last)
            last.then_inc(S["mixed"], 1)
            dve.wait_ge(S["mixed"], 2)
            gs = G[:, :, NP:NT].rearrange("p h (b t) -> p h b t", b=NSEQ)
            tt(T[0][:, :, NP:NT].rearrange("p h (b t) -> p h b t", b=NSEQ),
               gs[:, :, :, TS - 1:TS].to_broadcast([P, H, NSEQ, TS]), gs, ALU.subtract).then_inc(S["kd_sub"], 1)
            dve.wait_ge(S["kd_exp"], H + 1)
            tt(T[0][:, :, :], T[0][:, :, :], KB[:, :, :], ALU.mult).then_inc(S["kd_ok"], 1)
            dve.wait_ge(S["kat_mm"], 1)
            for i, (_, r) in enumerate(TILES):
                src = ps[0:r, 5 + i // 2, (i % 2) * 256:(i % 2) * 256 + 256]
                tt(KAt[0:r, i, :].rearrange("p (h d) -> p h d", h=H), src.rearrange("p (h d) -> p h d", h=H),
                   cols[0:r, i, 1, :].unsqueeze(2).to_broadcast([r, H, DKA]), ALU.mult).then_inc(S["kat_ok"], 1)

            dve.wait_ge(S["slots_used"], OUT_SLOT0 + KT)
            dve.wait_ge(S["ln2_in"], 32)
            for i, (_, r) in enumerate(TILES):
                for half in range(2):
                    x = xs[0:r, i, half * 512:(half + 1) * 512]
                    stt(x, x, ALPHA, out_banks(i, half), ALU.mult, ALU.add).then_inc(S["r1_ok"], 1)
            dve.wait_ge(S["r1_ok"], 6)
            for i in range(3):
                norm(i, 4 + i)

            def split(i):
                r = TILES[i][1]
                tmp, x = split_tmp[0:r, :], xs[0:r, i, :]
                step(nc.vector.tensor_copy(xb[i][0:r, :], x))
                step(tt(tmp, x, xb[i][0:r, :], ALU.subtract))
                step(nc.vector.tensor_copy(xb[3 + i][0:r, :], tmp))
                step(tt(xb[6 + i][0:r, :], tmp, xb[3 + i][0:r, :], ALU.subtract))

            split(0)
            split(1)
            for i, (_, r) in enumerate(TILES):
                if i == 1:
                    split(2)
                dve.wait_ge(S["router_mm"], i + 1)
                tt(logit[0:r, :], ps[0:r, (4, 7, 4)[i], 0:NE], br[0:r, :], ALU.add).then_inc(S["logits_ok"], 1)
                dve.wait_ge(S["logits_ok"], i + 1)
                step(nc.vector.max(top_v[0:r, i, :], logit[0:r, :]))
                step(nc.vector.max_index(top_i[0:r, i, :], top_v[0:r, i, :], logit[0:r, :]))
                ts(neg_v[0:r, i:i + 1], top_v[0:r, i, 0:1], -1.0, None, ALU.mult).then_inc(S["top_ok"], 1)
                step(nc.vector.tensor_copy(top_f[0:r, i, :], top_i[0:r, i, :]))
                step(tt(oneh[0:r, i, :, :], iota[0:r, :].unsqueeze(1).to_broadcast([r, TOPK, NE]),
                        top_f[0:r, i, 0:TOPK].unsqueeze(2).to_broadcast([r, TOPK, NE]), ALU.is_equal))
                nc.vector.tensor_reduce(pick[0:r, i, :], oneh[0:r, i, :, :].rearrange("p k e -> p e k"),
                                        axis=AX_X, op=ALU.add).then_inc(S["pick_ok"], 1)
            dve.wait_ge(S["rank_mm"], 1)
            step(tt(row_of[:, :, 0:NE], ps[:, 4, P:P + 3 * NE].rearrange("p (i e) -> p i e", i=3), pick[:, :, :], ALU.mult))
            step(ts(row_of[:, :, 0:NE], row_of[:, :, 0:NE], -1.0, None, ALU.add))
            step(nc.vector.tensor_copy(ex[:, 3, :], ps[:, 4, P + 3 * NE:P + 4 * NE]))

            def one_hot(e):
                tt(OH[:, :, :], rows_iota.unsqueeze(1).to_broadcast([P, 3, BLK]),
                   row_of[:, :, bass.ds(e, 1)].to_broadcast([P, 3, BLK]), ALU.is_equal).then_inc(S["OH_ok"], 1)

            def gate_matrix(e):
                for i in range(3):
                    last = stt(GW[:, i, :], rows_iota, row_of[:, i, bass.ds(e, 1)],
                               gate_of[:, i, bass.ds(e, 1)].to_broadcast([P, BLK]), ALU.is_equal, ALU.mult)
                last.then_inc(S["GW_ok"], 1)

            one_hot(0)
            def selector(b):
                ts(sel[:, :], cf[0:3 * NE, CF_PMOD:CF_PMOD + BLK], blk_e[0:3 * NE, bass.ds(b, 1)], None,
                   ALU.is_equal).then_inc(S["sel_ok"], 1)

            def add_shares(b):
                for n, bank in enumerate(CB_BANKS):
                    dve.wait_ge(S["cb_mm"], b * 5 + (n + 1))
                    i, half = (n // 2, n % 2) if n < 4 else (2, 0)
                    for half in (0, 1) if n == 4 else (half,):
                        r = TILES[i][1]
                        lo = 64 * half if n == 4 else 0
                        x = xs[0:r, i, half * 512:(half + 1) * 512]
                        last = tt(x, x, ps[lo:lo + r, bank, :], ALU.add)
                    last.then_inc(S["cb_added"], 1)

            def expert_block(b, ahead, last_block=None, tile=None):
                if not ahead and last_block is not None:
                    add_shares(last_block)
                dve.wait_ge(S["slots_used"], b * PER + (PRE + 2 * KT))
                ts(g_s, ps[:, 0, :], LIMIT, None, ALU.min).then_inc(S["g_ready"], 1)
                ts(u_s, ps[:, 1, :], LIMIT, -LIMIT, ALU.min, ALU.max).then_inc(S["gu_free"], 1)
                dve.wait_ge(S["g_ready"], b + 1)
                dve.wait_ge(S["gu_free"], b + 2)
                stt(u_s, u_s, 1.0, g_s, ALU.add, ALU.mult).then_inc(S["ug_ok"], 1)
                dve.wait_ge(S["ug_ok"], b + 1)
                dve.wait_ge(S["sg_ok"], b + 1)
                tt(h_s, u_s, sg_s, ALU.mult).then_inc(S["h_ok"], 1)
                if ahead and last_block is not None:
                    add_shares(last_block)
                if ahead:
                    dve.wait_ge(S["rows_mm"], b + 2)
                    one_hot(b + 2)
                    dve.wait_ge(S["gt_mm"], b + 1)
                    gate_matrix(b + 1)
                    dve.wait_ge(S["slots_used"], b * PER + (PRE + 2 * KT + 1))
                    selector(b + 1)
                if tile is not None:
                    dve.wait_ge(S["ple_sig"], tile + 1)
                    tt(ple, ple, ps[:, 6, 0:NT], ALU.mult).then_inc(S["ple_prod"], 1)
                    dve.wait_ge(S["ple_t"], tile + 1)
                    for i, (_, r) in enumerate(TILES):
                        x = xs[0:r, i, bass.ds(tile * P, P)]
                        last = tt(x, x, ps[0:r, 2, i * P:(i + 1) * P], ALU.add)
                    last.then_inc(S["ple_added"], 1)

            selector(0)
            dve.sem_inc(S["gu_free"], 1)
            dve.wait_ge(S["gate_exp"], 3)
            for i, (_, r) in enumerate(TILES):
                step(nc.vector.reciprocal(gsum[0:r, i:i + 1], gsum[0:r, i:i + 1]))
                step(ts(gate[0:r, i, :], gate[0:r, i, :], gsum[0:r, i:i + 1], None, ALU.mult))
            for i in range(3):
                sel4 = ext[:, 0:TOPK, :]
                step(tt(sel4, oneh[:, i, :, :], gate[:, i, :].unsqueeze(2).to_broadcast([P, TOPK, NE]), ALU.mult))
                step(nc.vector.tensor_reduce(gate_of[:, i, 0:NE], sel4.rearrange("p k e -> p e k"), axis=AX_X, op=ALU.add))
            gate_matrix(0)
            dve.wait_ge(S["rows_mm"], 1)
            one_hot(1)
            step(ts(ex[:, 0, :], ex[:, 3, :], float(CHUNKS[0]), None, ALU.is_gt))
            for c in CHUNKS[1:]:
                step(stt(ex[:, 0, :], ex[:, 3, :], float(c), ex[:, 0, :], ALU.is_gt, ALU.add))
            step(nc.vector.tensor_tensor_scan(ex[:, 1, :], ones[:, 0:NE], ex[:, 0, :], 0.0, ALU.mult, ALU.add))
            step(tt(ext[:, :, :], ex[:, 1, :].unsqueeze(1).to_broadcast([P, NEXTRA, NE]),
                    iota[:, 0:NEXTRA].unsqueeze(2).to_broadcast([P, NEXTRA, NE]), ALU.is_le))
            step(nc.vector.tensor_reduce(blk_e[:, NE:NBLK], ext[:, :, :], axis=AX_X, op=ALU.add))
            step(nc.vector.tensor_copy(blk_ei[:, :], blk_e[:, :]))
            nc.vector.tensor_copy(n_exti[:, :], ex[:, 1, NE - 1:NE]).then_inc(S["pos_ok"], 1)
            for i, (_, r) in enumerate(TILES):
                step(ts(xs[0:r, i, :], xs[0:r, i, :], ALPHA, None, ALU.mult))
            dve.sem_inc(S["ple_added"], 1)
            for b in range(HEAD_BLOCKS):
                expert_block(b, True, b - 1 if b else None)
            with dve.Fori(0, KT) as c:
                expert_block(c * 2 + HEAD_BLOCKS, True, c * 2 + (HEAD_BLOCKS - 1))
                expert_block(c * 2 + (HEAD_BLOCKS + 1), True, c * 2 + HEAD_BLOCKS, c)
            with dve.Fori(PLE_END, NE - 1) as b:
                expert_block(b, True, b - 1)
            expert_block(NE - 1, False, NE - 2)
            add_shares(NE - 1)
            extra = dve.value_load(n_exti[0:1, 0:1], min_val=0, max_val=NEXTRA)
            with dve.If(extra > 0):
                with dve.Fori(0, NEXTRA) as j:
                    with dve.If(extra > j):
                        e = dve.value_load(blk_ei[0:1, bass.ds(j + NE, 1)], min_val=0, max_val=NE - 1)
                        dve.wait_ge(S["cb_added"], j * 5 + 5 * NE)
                        ts(row_of[:, :, bass.ds(e, 1)], row_of[:, :, bass.ds(e, 1)], -float(BLK), None,
                           ALU.add).then_inc(S["row_moved"], 1)
                        dve.wait_ge(S["row_moved"], j + 1)
                        one_hot(e)
                        gate_matrix(e)
                        selector(j + NE)
                        expert_block(j + NE, False)
                        add_shares(j + NE)

            dve.wait_ge(S["ln3_in"], 32)
            dve.wait_ge(S["cb_added"], extra * 5 + 5 * NE)
            for i in range(3):
                norm_stats(i, 7 + i)
            for i in range(3):
                norm_apply(i, 7 + i)


_INS = ["x_prompt", "x_sample", "state_mlstm_C", "state_mlstm_n", "state_mlstm_m", "state_hgrn_S", "p_prompt",
        "p_sample", "ln_in_g", "ln_in_b", "w_in", "mlstm_ig_bias", "mlstm_fg_bias", "mlstm_norm_g",
        "hgrn_lb_logits", "hgrn_norm_g", "w_out", "ln1_g", "ln1_b", "w_router", "b_router", "w_gate", "b_gate",
        "w_up", "b_up", "w_down", "b_down", "w_ple_gate", "w_ple_proj", "ln2_g", "ln2_b"]
_OUTS = [(1, 256, 1024), (8, 4, 1024), (1, 1, 4, 64, 128), (1, 1, 4, 64), (1, 1, 4), (1, 1, 4, 128, 128),
         (1, 8, 4, 64, 128), (1, 8, 4, 64), (1, 8, 4), (1, 8, 4, 128, 128)]


def kernel(**inputs):
    import numpy as _np
    import concourse.bacc as _bacc
    from concourse import mybir as _mybir
    from concourse.bass_utils import run_bass_kernel_spmd as _run

    nc = _bacc.Bacc("TRN2", target_bir_lowering=False, num_devices=1)
    arrays, aps = {}, {}
    given = [(n, inputs[n]) for n in _INS] + list(zip(("const_f", "const_m"), constant_arrays()))
    for name, value in given:
        v = _np.ascontiguousarray(value)
        arrays[f"in_{name}"] = v
        aps[name] = nc.dram_tensor(f"in_{name}", v.shape, _mybir.dt.from_np(v.dtype), kind="ExternalInput").ap()
    outs = [nc.dram_tensor(f"out_{n}", shape, _mybir.dt.float32, kind="ExternalOutput").ap()
            for n, shape in enumerate(_OUTS)]
    trunk_step(nc, aps, outs)
    r = _run(nc, [arrays], core_ids=[0])
    return tuple(r.results[0][f"out_{n}"] for n in range(len(_OUTS)))
```
